# Optimizing a Trainium2 kernel written in Bass

```python
import jax, jax.numpy as jnp
from jax import lax
import numpy as np

D_MODEL = 1024
BATCH = 1
SEQ = 512
DEPTH = 2

CHUNK = 64
N_MIXERS = 2
N_A = (DEPTH + 1) // 2
N_B = DEPTH // 2
FOX_HEADS = 16
FOX_HEAD_DIM = D_MODEL // FOX_HEADS
Q_BLOCK = 128
RNN_WIDTH = (4 * D_MODEL // 3) // 128 * 128
RNN_BLOCKS = 16
RNN_BLOCK_W = RNN_WIDTH // RNN_BLOCKS
CONV_WIDTH = 4
RG_C = 8.0
D_FF = (8 * D_MODEL // 3 + 255) // 256 * 256
RMS_EPS = 1e-6

kernel_name = "fox_rglru_macaron_hybrid"

def rmsnorm(x, g):
    xf = x.astype(jnp.float32)
    y = xf * lax.rsqrt(jnp.mean(xf * xf, axis=-1, keepdims=True) + RMS_EPS)
    return (y * g.astype(jnp.float32)).astype(x.dtype)

def swiglu(h, w_gu, w_down):
    g, u = jnp.split(h @ w_gu, 2, axis=-1)
    return (jax.nn.silu(g) * u) @ w_down

def forgetting_attention_mixer(h, w_in, b_f, w_out):
    B, T, _ = h.shape
    proj = h @ w_in
    q, k, v, f_logit = jnp.split(proj, [D_MODEL, 2 * D_MODEL, 3 * D_MODEL], axis=-1)
    q = q.reshape(B, T, FOX_HEADS, FOX_HEAD_DIM)
    k = k.reshape(B, T, FOX_HEADS, FOX_HEAD_DIM)
    v = v.reshape(B, T, FOX_HEADS, FOX_HEAD_DIM)
    log_f = jax.nn.log_sigmoid(f_logit.astype(jnp.float32) + b_f.astype(jnp.float32))
    F = jnp.transpose(jnp.cumsum(log_f, axis=1), (0, 2, 1))
    scale = FOX_HEAD_DIM ** -0.5
    k_pos = jnp.arange(T)

    def q_block(i):
        start = i * Q_BLOCK
        qb = lax.dynamic_slice_in_dim(q, start, Q_BLOCK, axis=1)
        Fq = lax.dynamic_slice_in_dim(F, start, Q_BLOCK, axis=2)
        s = jnp.einsum('bqhd,bkhd->bhqk', qb, k, preferred_element_type=jnp.float32) * scale
        s = s + Fq[..., :, None] - F[..., None, :]
        q_pos = start + jnp.arange(Q_BLOCK)
        s = jnp.where(k_pos[None, :] <= q_pos[:, None], s, -jnp.inf)
        p = jax.nn.softmax(s, axis=-1)
        return jnp.einsum('bhqk,bkhd->bqhd', p.astype(v.dtype), v)

    out = lax.map(q_block, jnp.arange(T // Q_BLOCK))
    out = jnp.moveaxis(out, 0, 1).reshape(B, T, D_MODEL)
    return out @ w_out

def _lru_combine(c1, c2):
    a1, b1 = c1
    a2, b2 = c2
    return a1 * a2, a2 * b1 + b2

def rglru_mixer(h, w_in, conv_w, conv_b, w_a, b_a, w_i, b_i, lam, w_out):
    B, T, _ = h.shape
    gate_br, rec_br = jnp.split(h @ w_in, 2, axis=-1)
    gate_br = jax.nn.gelu(gate_br)
    xp = jnp.pad(rec_br, ((0, 0), (CONV_WIDTH - 1, 0), (0, 0)))
    xc = conv_b + xp[:, 0:T] * conv_w[0]
    for j in range(1, CONV_WIDTH):
        xc = xc + xp[:, j:j + T] * conv_w[j]
    xb = xc.reshape(B, T, RNN_BLOCKS, RNN_BLOCK_W)
    r = jax.nn.sigmoid((jnp.einsum('btnc,ncd->btnd', xb, w_a).reshape(B, T, RNN_WIDTH) + b_a).astype(jnp.float32))
    gi = jax.nn.sigmoid((jnp.einsum('btnc,ncd->btnd', xb, w_i).reshape(B, T, RNN_WIDTH) + b_i).astype(jnp.float32))
    log_a = -RG_C * r * jax.nn.softplus(-lam.astype(jnp.float32))
    a = jnp.exp(log_a)
    b = jnp.sqrt(-jnp.expm1(2.0 * log_a)) * (gi * xc.astype(jnp.float32))
    _, hs = lax.associative_scan(_lru_combine, (a, b), axis=1)
    y = hs.astype(h.dtype) * gate_br
    return y @ w_out

def _normal(key, shape, fan_in):
    return jax.random.normal(key, shape, jnp.float32) * (fan_in ** -0.5)

def _gain(key, shape):
    return 1.0 + 0.05 * jax.random.normal(key, shape, jnp.float32)

def setup_inputs(seed: int = 0) -> dict:
    key = jax.random.key(seed)
    ks = jax.random.split(key, 24)
    D, R = D_MODEL, RNN_WIDTH
    a0 = jax.random.uniform(ks[20], (N_B, R), jnp.float32, 0.9, 0.999)
    s0 = a0 ** (1.0 / RG_C)
    return {
        "x": jax.random.normal(ks[0], (BATCH, SEQ, D), jnp.float32),
        "ffn1_norm": _gain(ks[1], (DEPTH, D)),
        "ffn1_w_gu": _normal(ks[2], (DEPTH, D, 2 * D_FF), D),
        "ffn1_w_down": _normal(ks[3], (DEPTH, D_FF, D), D_FF),
        "mix_norm": _gain(ks[4], (DEPTH, D)),
        "ffn2_norm": _gain(ks[5], (DEPTH, D)),
        "ffn2_w_gu": _normal(ks[6], (DEPTH, D, 2 * D_FF), D),
        "ffn2_w_down": _normal(ks[7], (DEPTH, D_FF, D), D_FF),
        "fox_w_in": _normal(ks[8], (N_A, D, 3 * D + FOX_HEADS), D),
        "fox_b_f": 2.0 + 0.5 * jax.random.normal(ks[9], (N_A, FOX_HEADS), jnp.float32),
        "fox_w_out": _normal(ks[10], (N_A, D, D), D),
        "lru_w_in": _normal(ks[11], (N_B, D, 2 * R), D),
        "lru_conv_w": _normal(ks[12], (N_B, CONV_WIDTH, R), CONV_WIDTH),
        "lru_conv_b": 0.02 * jax.random.normal(ks[13], (N_B, R), jnp.float32),
        "lru_w_a": _normal(ks[14], (N_B, RNN_BLOCKS, RNN_BLOCK_W, RNN_BLOCK_W), RNN_BLOCK_W),
        "lru_b_a": 0.02 * jax.random.normal(ks[15], (N_B, R), jnp.float32),
        "lru_w_i": _normal(ks[16], (N_B, RNN_BLOCKS, RNN_BLOCK_W, RNN_BLOCK_W), RNN_BLOCK_W),
        "lru_b_i": 0.02 * jax.random.normal(ks[17], (N_B, R), jnp.float32),
        "lru_lambda": jnp.log(s0) - jnp.log1p(-s0),
        "lru_w_out": _normal(ks[18], (N_B, R, D), R),
        "final_norm": _gain(ks[19], (D,)),
    }

def reference(x, ffn1_norm, ffn1_w_gu, ffn1_w_down, mix_norm, ffn2_norm, ffn2_w_gu, ffn2_w_down,
              fox_w_in, fox_b_f, fox_w_out, lru_w_in, lru_conv_w, lru_conv_b, lru_w_a, lru_b_a,
              lru_w_i, lru_b_i, lru_lambda, lru_w_out, final_norm):
    for i in range(DEPTH):
        x = x + 0.5 * swiglu(rmsnorm(x, ffn1_norm[i]), ffn1_w_gu[i], ffn1_w_down[i])
        h = rmsnorm(x, mix_norm[i])
        j = i // N_MIXERS
        if i % N_MIXERS == 0:
            m = forgetting_attention_mixer(h, fox_w_in[j], fox_b_f[j], fox_w_out[j])
        else:
            m = rglru_mixer(h, lru_w_in[j], lru_conv_w[j], lru_conv_b[j], lru_w_a[j], lru_b_a[j],
                            lru_w_i[j], lru_b_i[j], lru_lambda[j], lru_w_out[j])
        x = x + m
        x = x + 0.5 * swiglu(rmsnorm(x, ffn2_norm[i]), ffn2_w_gu[i], ffn2_w_down[i])
    return rmsnorm(x, final_norm)


_drawn_inputs = setup_inputs


def setup_inputs(seed=0):
    import zlib

    import numpy as np

    out = dict(_drawn_inputs(seed))
    spreads = {}
    factors = {'lru_b_a': 34.257, 'lru_b_i': 21.804}
    for name, (base, spread) in spreads.items():
        noise = np.random.default_rng([zlib.crc32(name.encode()), seed]).standard_normal(out[name].shape)
        drawn = base * np.exp(spread * noise) if base else spread * noise
        out[name] = __import__('jax').numpy.asarray(drawn.astype(out[name].dtype))
    for name, factor in factors.items():
        out[name] = (out[name] * factor).astype(out[name].dtype)
    return out
```

```python
from contextlib import ExitStack

import numpy as np

import concourse.bass as bass
from concourse import mybir

F32 = mybir.dt.float32
F32R = mybir.dt.float32r
ALU = mybir.AluOpType
ACT = mybir.ActivationFunctionType
AX = mybir.AxisListType
ts = bass.ts

P = 128
T = 512
D = 1024
DEPTH = 2
HEADS = 16
HEAD_DIM = D // HEADS
R = (4 * D // 3) // 128 * 128
LRU_BLOCKS = 16
LRU_BLOCK = R // LRU_BLOCKS
TAPS = 4
RG_C = 8.0
D_FF = (8 * D // 3 + 255) // 256 * 256
EPS = 1e-6

KD = D // P
KF = D_FF // P
KR = R // P
TT = T // P
HALF_F = KF // 2
N_FFN = 2 * DEPTH
N_NORMS = 3 * DEPTH + 1
MASKED = -1e30

GATE_HALF = 5
BAND = [[i for i in range(KR)
         if any(b * LRU_BLOCK < (m + 1) * P and (b + 1) * LRU_BLOCK > m * P
                and b * LRU_BLOCK < (i + 1) * P and (b + 1) * LRU_BLOCK > i * P
                for b in range(LRU_BLOCKS))] for m in range(KR)]
GATE_BLOCKS = sum(len(BAND[m]) for m in range(GATE_HALF))

COL_GAIN = 0
COL_CONV_W = COL_GAIN + N_NORMS * KD
COL_CONV_B = COL_CONV_W + TAPS * KR
COL_B_A = COL_CONV_B + KR
COL_B_I = COL_B_A + KR
COL_LAMBDA = COL_B_I + KR
COL_B_F = COL_LAMBDA + KR
N_PARAMS = COL_B_F + 1

PAIR = 2 * KD * P
DOWN = HALF_F * P
STREAM = [
    ("gu0", KF, PAIR), ("down0", 2 * KD, DOWN),
    ("qk", KD, PAIR), ("f", 1, KD * P), ("v", 4, PAIR), ("fox_out", KD // 2, PAIR),
    ("gu1", KF, PAIR), ("down1", 2 * KD, DOWN),
    ("gu2", KF, PAIR), ("down2", 2 * KD, DOWN),
    ("rec", KR // 2, PAIR), ("gates", 4, GATE_BLOCKS * P), ("gate_br", KR // 2, PAIR),
    ("lru_out", KD, KR * P),
    ("gu3", KF, PAIR), ("down3", 2 * KD, DOWN),
]
BASE, COLS, UNIT_COLS = {}, {}, []
for _kind, _n, _cols in STREAM:
    BASE[_kind], COLS[_kind] = len(UNIT_COLS), _cols
    UNIT_COLS += [_cols] * _n
N_UNITS = len(UNIT_COLS)

PAIR_BASE, _q = {}, 0
for _kind, _n, _cols in STREAM:
    if _kind in ("qk", "fox_out", "rec", "gate_br") or _kind.startswith("gu"):
        PAIR_BASE[_kind] = _q
        _q += _n
FREED = {"gu0": 0, "qk": KF, "gu1": KF + KD, "gu2": 2 * KF + KD, "gu3": 3 * KF + KD}


def build_trunk(nc, x_t, params, gu, down, qk, f_w, v_w, fox_out, rec, gates, gate_br, lru_out, out_t):
    ctx = ExitStack()
    with ctx:
        base = (nc.sbuf_base + 31) // 32 * 32
        nc_room = nc.sbuf_bytes_remaining
        ctx.enter_context(nc.sbuf_tensor("slab", [P, (nc.sbuf_bytes_remaining - 64) // 4], F32))
        end = [0]

        def place(at, name, cols, dt=F32, parts=P):
            return nc.alloc_sbuf_tensor_at(name, [parts, cols], dt, offset=base + 4 * at)

        def area(cols):
            at = end[0]
            end[0] = at + (cols + 7) // 8 * 8
            return at

        def sb(name, cols, dt=F32, parts=P):
            return place(area(cols), name, cols, dt, parts)

        def sem(name):
            return ctx.enter_context(nc.semaphore(name))

        x = sb("x", KD * T)
        w_raw = [sb(f"w_raw{i}", PAIR) for i in range(2)]
        w_hi = [sb(f"w_hi{i}", PAIR, F32R) for i in range(2)]
        w_lo = [sb(f"w_lo{i}", PAIR, F32R) for i in range(2)]
        par = sb("par", N_PARAMS)
        r_bc = sb("r_bc", T)
        ssq = sb("ssq", T)
        sq_at = area(2 * T)
        sq = place(sq_at, "sq", 2 * T)
        ones = sb("ones", P)
        ident = sb("ident", P)
        ident_r = sb("ident_r", P, F32R)
        mask_r = sb("mask_r", P, F32R)
        eps = sb("eps", 1)
        r_tok = sb("r_tok", TT)
        lru_c = sb("lru_c", KR)
        lru_nc = sb("lru_nc", KR)
        sp = sb("sp", 6 * KR)
        neg_max = sb("neg_max", 2 * TT)
        row_sum = sb("row_sum", 2 * TT)
        row_rcp = sb("row_rcp", 2 * TT)

        xg_area = area(2 * KD * T)
        h_area = area(2 * KF * T)
        t_area = area(4 * T)
        assert 4 * end[0] + 64 <= nc_room, (4 * end[0], nc_room)

        xg_hi = place(xg_area, "xg_hi", KD * T, F32R)
        xg_lo = place(xg_area + KD * T, "xg_lo", KD * T, F32R)
        h_hi = place(h_area, "h_hi", KF * T, F32R)
        h_lo = place(h_area + KF * T, "h_lo", KF * T, F32R)
        g_buf = [place(t_area + i * T, f"g_buf{i}", T) for i in range(2)]
        u_buf = [place(t_area + (2 + i) * T, f"u_buf{i}", T) for i in range(2)]
        q_raw = place(h_area, "q_raw", KD * T)
        k_raw = place(h_area + KD * T, "k_raw", KD * T)
        o_hi = place(h_area, "o_hi", KD * T, F32R)
        o_lo = place(h_area + KD * T, "o_lo", KD * T, F32R)
        at = 2 * KD * T
        v_raw = place(h_area + at, "v_raw", TT * D)
        at += TT * D
        head = [place(h_area + at + i * 4 * T, f"head{i}", 4 * T, F32R, HEAD_DIM + 2) for i in range(2)]
        at += 8 * T
        PROB_COLS = P * TT * (TT + 1) // 2
        prob = [place(h_area + at + i * PROB_COLS, f"prob{i}", PROB_COLS) for i in range(2)]
        at += 2 * PROB_COLS
        v_hi = [place(h_area + at + i * T, f"v_hi{i}", TT * P, F32R) for i in range(2)]
        v_lo = [place(h_area + at + (2 + i) * T, f"v_lo{i}", TT * P, F32R) for i in range(2)]
        at += 4 * T
        one_zero = place(h_area + at, "one_zero", 2 * T, F32R, 1)
        pt_hi = [place(xg_area + (2 * i) * TT * T, f"pt_hi{i}", TT * T, F32R) for i in range(2)]
        pt_lo = [place(xg_area + (2 * i + 1) * TT * T, f"pt_lo{i}", TT * T, F32R) for i in range(2)]
        f_pack = place(t_area, "f_pack", 4 * T, F32R, HEADS)
        head_tmp = place(sq_at, "head_tmp", 2 * T)
        fl_a = place(h_area + 2 * KD * T + TT * D, "fl_a", T, F32, HEADS)
        fl_b = place(h_area + 2 * KD * T + TT * D + T, "fl_b", T, F32, HEADS)
        fl_c = place(h_area + 2 * KD * T + TT * D + 2 * T, "fl_c", T, F32, HEADS)
        r_gate = place(h_area, "r_gate", KR * T)
        xc = place(h_area + KR * T, "xc", KR * T)
        xc_hi = place(h_area + 2 * KR * T, "xc_hi", KR * T, F32R)
        xc_lo = place(h_area + 3 * KR * T, "xc_lo", KR * T, F32R)
        q_lru = place(h_area + 2 * KR * T, "q_lru", KR * T)
        gt = place(h_area + 3 * KR * T, "gt", KR * T)
        rec_pad = [place(t_area + i * (T + 8), f"rec_pad{i}", T + TAPS - 1) for i in range(2)]
        den = place(t_area + 2 * (T + 8), "den", T)
        gi = [place(sq_at + i * T, f"gi{i}", T) for i in range(2)]

        ps = [ctx.enter_context(nc.psum_tensor(f"ps{b}", [P, T], F32)) for b in range(8)]
        BANK_DOWN, BANK_SSQ, BANK_TOK, BANK_F = 4, 6, 7, 5
        BANK_PT, BANK_O, BANK_GATE, BANK_V = 4, 6, 4, 4

        par_in = sem("par_in")
        x_tile_in = [sem(f"x_tile_in{k}") for k in range(KD)]
        raw_in = [sem(f"raw_in{i}") for i in range(2)]
        hi_done = sem("hi_done")
        unit_ready = sem("unit_ready")
        unit_done = sem("unit_done")
        pair_free = sem("pair_free")
        x_new = sem("x_new")
        xg_hi_done = sem("xg_hi_done")
        xg_ready = sem("xg_ready")
        sq_done = sem("sq_done")
        ssq_added = sem("ssq_added")
        ssq_mm = sem("ssq_mm")
        sqrt_done = sem("sqrt_done")
        r_ready = sem("r_ready")
        ssq_zero = sem("ssq_zero")
        consts = sem("consts")
        g_ready = sem("g_ready")
        silu_done = sem("silu_done")
        h_made = sem("h_made")
        h_hi_done = sem("h_hi_done")
        h_ready = sem("h_ready")
        tok_mm = sem("tok_mm")
        tok_sqrt = sem("tok_sqrt")
        tok_ready = sem("tok_ready")
        f_step = sem("f_step")
        f_exp = sem("f_exp")
        f_packed = sem("f_packed")
        rows_in = [sem(f"rows_in{i}") for i in range(2)]
        v_raw_done = sem("v_raw_done")
        q_tmp = sem("q_tmp")
        k_tmp = sem("k_tmp")
        head_hi = sem("head_hi")
        head_ready = sem("head_ready")
        v_hi_done = sem("v_hi_done")
        v_ready = sem("v_ready")
        scores_done = sem("scores_done")
        max_done = sem("max_done")
        exp_done = sem("exp_done")
        rcp_done = sem("rcp_done")
        prob_ready = sem("prob_ready")
        pt_done = sem("pt_done")
        pt_hi_done = sem("pt_hi_done")
        pt_ready = sem("pt_ready")
        pv_done = sem("pv_done")
        o_hi_done = sem("o_hi_done")
        o_ready = sem("o_ready")
        lam_exp = sem("lam_exp")
        lam_step = sem("lam_step")
        rec_ready = sem("rec_ready")
        conv_step = sem("conv_step")
        tap0_done = sem("tap0_done")
        xc_hi_done = sem("xc_hi_done")
        xc_ready = sem("xc_ready")
        gate_mm = sem("gate_mm")
        gate_out = sem("gate_out")
        gi_used = sem("gi_used")
        tanh_done = sem("tanh_done")
        a_done = sem("a_done")
        q_step = sem("q_step")
        q_done = sem("q_done")
        root_done = sem("root_done")
        b_done = sem("b_done")
        scan_done = sem("scan_done")
        gt_ready = sem("gt_ready")
        gelu_done = sem("gelu_done")
        y_made = sem("y_made")
        y_hi_done = sem("y_hi_done")
        y_ready = sem("y_ready")
        out_made = sem("out_made")
        out_in_dram = sem("out_in_dram")

        def gain(n, m):
            return par[:, bass.ds(m + (COL_GAIN + n * KD), 1)]

        def col(base, m):
            return par[:, base + m:base + m + 1]

        def f32(ap):
            return ap.bitcast(F32)

        def rolled(eng, n, body, first=0, last=0, unroll=2):
            for k in range(first):
                body(k, k % unroll)
            turns = (n - first - last) // unroll
            if turns > 0:
                with eng.Fori(0, turns) as i:
                    for s in range(unroll):
                        body(i * unroll + (first + s), (first + s) % unroll)
            for k in range(first + max(turns, 0) * unroll, n):
                body(k, k % unroll)

        def pair_of(h):
            return h // 2

        block = ctx.enter_context(nc.Block())

        @block.sync
        def _(sp_):
            sp_.dma_start(par[:], params).then_inc(par_in, 16)
            for k in range(KD // 2):
                sp_.dma_start(x[:, ts(k, T)], x_t[k]).then_inc(x_tile_in[k], 16)

            def load(dram, base, cols):
                def body(k, s):
                    u = k + base
                    slot = (base + s) % 2
                    if not (isinstance(u, int) and u < 2):
                        sp_.wait_ge(unit_ready, u - 1)
                    sp_.dma_start(w_raw[slot][:, 0:cols],
                                  dram[bass.ds(k, 1)].rearrange("a p n -> (a p) n")).then_inc(raw_in[slot], 16)
                return body

            for kind, n, cols in STREAM:
                dram = {"qk": qk, "f": f_w, "v": v_w, "fox_out": fox_out, "rec": rec, "gates": gates,
                        "gate_br": gate_br, "lru_out": lru_out}.get(kind)
                if dram is None:
                    dram = (gu if kind.startswith("gu") else down)[int(kind[-1])]
                rolled(sp_, n, load(dram, BASE[kind], cols), first=2 if kind == "gu0" else 0)

            for m in range(KD):
                sp_.wait_ge(out_made, m + 1)
                sp_.dma_start(out_t[m], x[:, ts(m, T)]).then_inc(out_in_dram, 16)
            sp_.wait_ge(out_in_dram, 16 * KD)

        @block.gpsimd
        def _(pool):
            pool.memset(eps[:], EPS).then_inc(consts, 1)
            pool.memset(ones[:], 1.0).then_inc(consts, 1)
            pool.memset(ident[:], 1.0).then_inc(consts, 1)
            pool.memset(f32(mask_r[:]), 0.0).then_inc(consts, 1)
            pool.wait_ge(consts, 4)
            pool.affine_select(out=ident[:], in_=ident[:], compare_op=ALU.is_equal, fill=0.0, base=0,
                               pattern=[[-1, P]], channel_multiplier=1).then_inc(consts, 1)
            pool.affine_select(out=mask_r[:], in_=f32(mask_r[:]), compare_op=ALU.is_ge, fill=MASKED, base=0,
                               pattern=[[-1, P]], channel_multiplier=1).then_inc(consts, 1)
            pool.wait_ge(consts, 6)
            pool.tensor_copy(ident_r[:], ident[:]).then_inc(consts, 1)
            pool.sem_inc(pt_ready, 2)
            pool.sem_inc(pv_done, 2)
            pool.sem_inc(o_ready, 2)

            pool.wait_ge(f_packed, 1)
            for i in range(2):
                odd = head[i][:].rearrange("p (a b n) -> p a b n", a=2, b=2)
                src = one_zero[:].rearrange("p (a n) -> p a n", a=2)
                pool.dma_start(odd[HEAD_DIM:HEAD_DIM + 1, :, 1, :], src).then_inc(rows_in[i], 16)
                pool.dma_start(odd[HEAD_DIM + 1:HEAD_DIM + 2, :, 0, :], src).then_inc(rows_in[i], 16)

            def rows(h, s):
                if h >= 2:
                    pool.wait_ge(scores_done, (h - 1) * TT)
                slots = head[s][:].rearrange("p (a b n) -> p a b n", a=2, b=2)
                src = f_pack[h:h + 1, :].rearrange("p (a n) -> p a n", a=4)
                pool.dma_start(slots[HEAD_DIM:HEAD_DIM + 1, :, 0, :], src[:, 0:2, :]).then_inc(rows_in[s], 16)
                pool.dma_start(slots[HEAD_DIM + 1:HEAD_DIM + 2, :, 1, :], src[:, 2:4, :]).then_inc(rows_in[s], 16)

            for h in range(HEADS):
                rows(h, h % 2)

        @block.tensor
        def _(pe):
            def mm3(dst, a_hi, a_lo, b_hi, b_lo, start, stop):
                pe.matmul(dst, a_hi, b_hi, start=start, stop=False)
                pe.matmul(dst, a_hi, b_lo, start=False, stop=False)
                return pe.matmul(dst, a_lo, b_hi, start=False, stop=stop)

            def sum_squares(n):
                pe.wait_ge(ssq_added, KD * (n + 1))
                pe.matmul(ps[BANK_SSQ][:], ones[:], ssq[:], start=True, stop=True).then_inc(ssq_mm, 1)

            def pair_unit(base, pair_base, src_hi, src_lo, bank_free, ready=None, after_first=None):
                def body(j, s):
                    u = j + base
                    slot, bank = (base + s) % 2, 2 * ((pair_base + s) % 2)
                    first = isinstance(j, int) and j == 0
                    pe.wait_ge(unit_ready, u + 1)
                    bank_free(j)
                    for k in range(KD):
                        if first and ready:
                            ready(k)
                        for t in range(2):
                            b = ts(2 * k + t, P)
                            last = mm3(ps[bank + t][:], w_hi[slot][:, b], w_lo[slot][:, b],
                                       src_hi[:, ts(k, T)], src_lo[:, ts(k, T)], k == 0, k == KD - 1)
                    last.then_inc(unit_done, 1)
                    if first and after_first:
                        after_first()
                return body

            def after_two(sem_, before, per_unit):
                def wait(j):
                    if not (isinstance(j, int) and j < 2):
                        pe.wait_ge(sem_, j * per_unit + (before - per_unit))
                return wait

            def xg_wait(n):
                return lambda k: pe.wait_ge(xg_ready, KD * n + k + 1)

            def ffn(f, n):
                gu_k, down_k = f"gu{f}", f"down{f}"
                later = after_two(pair_free, FREED[gu_k], 1)

                def bank_free(j):
                    if f == 1 and isinstance(j, int) and j < 2:
                        pe.wait_ge(x_new, KD * n - KD + KD - 2 + 2 * j)
                    later(j)
                rolled(pe, KF, pair_unit(BASE[gu_k], PAIR_BASE[gu_k], xg_hi, xg_lo, bank_free, xg_wait(n),
                                         lambda: sum_squares(n)), first=2)

                def down_tile(m, s):
                    bank = BANK_DOWN + s
                    first = isinstance(m, int) and m == 0
                    for half in range(2):
                        u = m * 2 + (BASE[down_k] + half)
                        slot = (BASE[down_k] + half) % 2
                        pe.wait_ge(unit_ready, u + 1)
                        if half == 0 and not (isinstance(m, int) and m < 2):
                            pe.wait_ge(x_new, m + (KD * n - 1))
                        for kk in range(HALF_F):
                            k = half * HALF_F + kk
                            if first:
                                pe.wait_ge(h_ready, KF * f + k + 1)
                            last = mm3(ps[bank][:], w_hi[slot][:, ts(kk, P)], w_lo[slot][:, ts(kk, P)],
                                       h_hi[:, ts(k, T)], h_lo[:, ts(k, T)], k == 0, k == KF - 1)
                        last.then_inc(unit_done, 1)
                rolled(pe, KD, down_tile, first=2)

            def fox(n):
                def first_stats():
                    sum_squares(n)
                    for tt in range(TT):
                        last = pe.matmul(ps[BANK_TOK][:, tt:tt + 1], ssq[:, ts(tt, P)], ones[:, 0:1],
                                         start=True, stop=True)
                    last.then_inc(tok_mm, 1)
                rolled(pe, KD, pair_unit(BASE["qk"], PAIR_BASE["qk"], xg_hi, xg_lo,
                                         after_two(pair_free, FREED["qk"], 1), xg_wait(n), first_stats), first=2)
                u = BASE["f"]
                pe.wait_ge(unit_ready, u + 1)
                for k in range(KD):
                    last = mm3(ps[BANK_F][:], w_hi[u % 2][:, ts(k, P)], w_lo[u % 2][:, ts(k, P)],
                               xg_hi[:, ts(k, T)], xg_lo[:, ts(k, T)], k == 0, k == KD - 1)
                last.then_inc(unit_done, 1)
                for c in range(2):
                    for half in range(2):
                        u = BASE["v"] + 2 * c + half
                        pe.wait_ge(unit_ready, u + 1)
                        if c == 0 and half == 0:
                            pe.wait_ge(f_step, 1)
                            pe.wait_ge(r_ready, n + 1)
                            pe.wait_ge(tok_ready, 1)
                        if c == 1 and half == 0:
                            pe.wait_ge(pair_free, FREED["qk"] + KD)
                        for kk in range(KD // 2):
                            k = half * (KD // 2) + kk
                            for tt in range(TT):
                                at_ = slice(k * T + tt * P, k * T + (tt + 1) * P)
                                wc = ts(kk, T)
                                last = mm3(ps[BANK_V * (1 - c) + tt][:], xg_hi[:, at_], xg_lo[:, at_],
                                           w_hi[u % 2][:, wc], w_lo[u % 2][:, wc], k == 0, k == KD - 1)
                        last.then_inc(unit_done, 1)

                def scores(h, s, i):
                    b = s % 2
                    w = (i + 1) * P
                    rows = slice(0, HEAD_DIM + 2)
                    op = [head[b][rows, ts(a, T)] for a in range(4)]
                    if i == 0:
                        pe.wait_ge(head_ready, h + 1)
                        pe.wait_ge(rows_in[b], h * 16 + (64 - 16 * b))
                    if isinstance(h, int) and h == 0:
                        pe.wait_ge(v_raw_done, 2 * TT)
                    else:
                        pe.wait_ge(exp_done, (h - 1) * TT + (i + 1))
                    dst = ps[i][:, 0:w]
                    pe.matmul(dst, op[0][:, ts(i, P)], op[1][:, 0:w], start=True, stop=False)
                    pe.matmul(dst, op[0][:, ts(i, P)], op[3][:, 0:w], start=False, stop=False)
                    pe.matmul(dst, op[2][:, ts(i, P)], op[1][:, 0:w], start=False, stop=False)
                    pe.matmul(ps[i][:, i * P:w], ident_r[:], mask_r[:], start=False, stop=True)\
                        .then_inc(scores_done, 1)

                def transposes(h, s, j):
                    b = s % 2
                    if j == 0:
                        pe.wait_ge(prob_ready, (h + 1) * TT)
                    pe.wait_ge(pt_ready, h * TT + (j + 1))
                    for i in range(j, TT):
                        at_ = P * (i * (i + 1) // 2 + j)
                        last = pe.transpose(ps[BANK_PT + j % 2][:, ts(i, P)], prob[b][:, at_:at_ + P], ident[:])
                    last.then_inc(pt_done, 1)

                def values(h, s, j):
                    b, vb = s % 2, (s // 2) % 2
                    if j == 0:
                        pe.wait_ge(v_ready, pair_of(h) + 1)
                        pe.wait_ge(o_ready, h + 1)
                    pe.wait_ge(pt_ready, h * TT + (j + 3))
                    dst = ps[BANK_O + b][:, j * P:T]
                    kk = slice(j * T + j * P, (j + 1) * T)
                    last = mm3(dst, v_hi[vb][:, ts(j, P)], v_lo[vb][:, ts(j, P)], pt_hi[b][:, kk], pt_lo[b][:, kk],
                               j == 0, j == TT - 1)
                    if j == TT - 1:
                        last.then_inc(pv_done, 1)

                def attend(h, s):
                    more = not (isinstance(h, int) and h == HEADS - 1)
                    for j in range(TT):
                        if more:
                            scores(h + 1, s + 1, j)
                        transposes(h, s, j)
                        if j >= 1:
                            values(h, s, j - 1)
                    values(h, s, TT - 1)

                for i in range(TT):
                    scores(0, 0, i)
                rolled(pe, HEADS, attend, last=4, unroll=4)

                rolled(pe, KD // 2, pair_unit(BASE["fox_out"], PAIR_BASE["fox_out"], o_hi, o_lo,
                                              after_two(x_new, KD * n, 2),
                                              lambda k: pe.wait_ge(o_ready, 2 * (k + 1) + 2)), first=2)

            def lru(n):
                rolled(pe, KR // 2, pair_unit(BASE["rec"], PAIR_BASE["rec"], xg_hi, xg_lo, after_two(rec_ready, 0, 2),
                                              xg_wait(n), lambda: sum_squares(n)), first=2)
                g = 0
                for i in range(4):
                    u = BASE["gates"] + i
                    pe.wait_ge(unit_ready, u + 1)
                    blk = 0
                    for m0 in range(GATE_HALF):
                        m = (i // 2) * GATE_HALF + m0
                        if g >= 4:
                            pe.wait_ge(gate_out, g - 3)
                        elif g == 0:
                            pe.wait_ge(r_ready, n + 1)
                        pe.wait_ge(xc_ready, BAND[m][-1] + 1)
                        for t, k in enumerate(BAND[m]):
                            last = mm3(ps[BANK_GATE + g % 4][:], w_hi[u % 2][:, ts(blk, P)], w_lo[u % 2][:, ts(blk, P)],
                                       xc_hi[:, ts(k, T)], xc_lo[:, ts(k, T)], t == 0, t == len(BAND[m]) - 1)
                            blk += 1
                        last.then_inc(unit_done if m0 == GATE_HALF - 1 else gate_mm, 1)
                        g += 1
                rolled(pe, KR // 2, pair_unit(BASE["gate_br"], PAIR_BASE["gate_br"], xg_hi, xg_lo,
                                              after_two(gt_ready, 0, 2)), first=2)

                def out_tile(m, s):
                    u = m + BASE["lru_out"]
                    slot, bank = (BASE["lru_out"] + s) % 2, BANK_DOWN + s
                    pe.wait_ge(unit_ready, u + 1)
                    if isinstance(m, int) and m < 2:
                        pe.wait_ge(gate_out, 4 * GATE_HALF)
                    else:
                        pe.wait_ge(x_new, m + (KD * n - 1))
                    for k in range(KR):
                        if isinstance(m, int) and m == 0:
                            pe.wait_ge(y_ready, k + 1)
                        last = mm3(ps[bank][:], w_hi[slot][:, ts(k, P)], w_lo[slot][:, ts(k, P)],
                                   xc_hi[:, ts(k, T)], xc_lo[:, ts(k, T)], k == 0, k == KR - 1)
                    last.then_inc(unit_done, 1)
                rolled(pe, KD, out_tile, first=2)

            pe.wait_ge(consts, 7)
            ffn(0, 0)
            fox(1)
            ffn(1, 2)
            ffn(2, 3)
            lru(4)
            ffn(3, 5)
            sum_squares(N_NORMS - 1)

        @block.scalar
        def _(act):
            for k in range(KD // 2, KD):
                act.dma_start(x[:, ts(k, T)], x_t[k]).then_inc(x_tile_in[k], 16)

            def hi_split(u, cols, slot):
                if isinstance(u, int):
                    if u >= N_UNITS:
                        return
                    cols = UNIT_COLS[u]
                act.wait_ge(raw_in[slot], u * 8 + (16 - 8 * slot))
                if not (isinstance(u, int) and u < 2):
                    act.wait_ge(unit_done, u - 1)
                act.activation(w_hi[slot][:, 0:cols], w_raw[slot][:, 0:cols], ACT.Copy).then_inc(hi_done, 1)

            def x_tile(n, m, s):
                c = m + KD * n
                if not (isinstance(c, int) and c < 2):
                    act.wait_ge(ssq_added, c - 1)
                act.wait_ge(x_new, m + (KD * (n - 1) + 1))
                if n < N_NORMS - 1:
                    act.activation(xg_hi[:, ts(m, T)], x[:, ts(m, T)], ACT.Copy, scale=gain(n, m))\
                        .then_inc(xg_hi_done, 1)
                act.activation(sq[:, ts(s, T)], x[:, ts(m, T)], ACT.Square).then_inc(sq_done, 1)

            def root(n):
                act.wait_ge(ssq_mm, n + 1)
                act.activation(r_bc[:], ps[BANK_SSQ][:], ACT.Sqrt, scale=1.0 / D, bias=eps[:]).then_inc(sqrt_done, 1)

            def ffn(f, n):
                gu_k, down_k = f"gu{f}", f"down{f}"

                def gu_unit(j, s):
                    if isinstance(j, int) and j == 0:
                        root(n)
                    hi_split(j + (BASE[gu_k] + 2), PAIR, (BASE[gu_k] + s) % 2)
                    act.wait_ge(g_ready, j + (KF * f + 1))
                    act.activation(g_buf[s][:], g_buf[s][:], ACT.Silu).then_inc(silu_done, 1)
                rolled(act, KF, gu_unit, first=2, last=2)

                def down_tile(m, s):
                    u = m * 2 + (BASE[down_k] + 2)
                    hi_split(u, DOWN, BASE[down_k] % 2)
                    x_tile(n + 1, m, s)
                    hi_split(u + 1, DOWN, (BASE[down_k] + 1) % 2)
                rolled(act, KD, down_tile, last=2)

            def fox(n):
                def qk_unit(j, s):
                    if isinstance(j, int) and j == 0:
                        root(n)
                        act.wait_ge(tok_mm, 1)
                        act.activation(r_tok[:], ps[BANK_TOK][:, 0:TT], ACT.Sqrt, scale=1.0 / D, bias=eps[:])\
                            .then_inc(tok_sqrt, 1)
                    hi_split(j + (BASE["qk"] + 2), PAIR, (BASE["qk"] + s) % 2)
                rolled(act, KD, qk_unit, first=2, last=2)
                hi_split(BASE["f"] + 2, 0, BASE["f"] % 2)
                act.wait_ge(f_step, 2)
                act.activation(fl_b[:], fl_a[:], ACT.Abs).then_inc(f_exp, 1)
                act.wait_ge(f_exp, 1)
                act.activation(fl_b[:], fl_b[:], ACT.Exp, scale=-1.0).then_inc(f_exp, 1)
                act.wait_ge(f_exp, 2)
                act.activation(fl_b[:], fl_b[:], ACT.Ln, scale=1.0, bias=ones[0:HEADS, 0:1]).then_inc(f_exp, 1)
                for i in range(4):
                    u = BASE["v"] + i
                    hi_split(u + 2, 0, u % 2)
                    if i % 2 == 1:
                        c = i // 2
                        act.wait_ge(unit_done, u + 1)
                        act.wait_ge(tok_ready, 1)
                        for tt in range(TT):
                            act.activation(v_raw[:, tt * D + c * T:tt * D + (c + 1) * T], ps[BANK_V * (1 - c) + tt][:],
                                           ACT.Copy, scale=r_tok[:, tt:tt + 1]).then_inc(v_raw_done, 1)

                def v_split(pair, vb):
                    if not (isinstance(pair, int) and pair == 0):
                        act.wait_ge(pv_done, pair * 2)
                    act.wait_ge(v_raw_done, 2 * TT)
                    src = v_raw[:].rearrange("p (t n) -> p t n", t=TT)[:, :, ts(pair, P)]
                    act.activation(v_hi[vb][:].rearrange("p (t n) -> p t n", t=TT), src, ACT.Copy)\
                        .then_inc(v_hi_done, 1)

                def expand(h, s):
                    b, ro, pair = s % 2, HEAD_DIM * (s % 2), pair_of(h)
                    if isinstance(h, int) and h == 0:
                        act.wait_ge(tok_sqrt, 1)
                    else:
                        act.wait_ge(head_ready, h)
                    act.wait_ge(pair_free, FREED["qk"] + KD)
                    act.activation(head_tmp[0:HEAD_DIM, 0:T], q_raw[ro:ro + HEAD_DIM, ts(pair, T)], ACT.Copy,
                                   scale=HEAD_DIM ** -0.5).then_inc(q_tmp, 1)
                    act.wait_ge(q_tmp, h + 1)
                    act.wait_ge(k_tmp, h + 1)
                    if not (isinstance(h, int) and h < 2):
                        act.wait_ge(scores_done, (h - 1) * TT)
                    act.activation(head[b][0:HEAD_DIM, 0:2 * T], head_tmp[0:HEAD_DIM, :], ACT.Copy)\
                        .then_inc(head_hi, 1)

                def exp_block(h, s, i):
                    b = s % 2
                    w, at_ = (i + 1) * P, P * (i * (i + 1) // 2)
                    act.wait_ge(max_done, h * TT + (i + 1))
                    if not (isinstance(h, int) and h < 2):
                        act.wait_ge(pt_done, (h - 1) * TT)
                    act.activation(prob[b][:, at_:at_ + w], ps[i][:, 0:w], ACT.Exp,
                                   bias=neg_max[:, b * TT + i:b * TT + i + 1],
                                   accum_out=row_sum[:, b * TT + i:b * TT + i + 1]).then_inc(exp_done, 1)

                def attend(h, s):
                    more = not (isinstance(h, int) and h == HEADS - 1)
                    b = s % 2
                    for j in range(TT):
                        if more:
                            exp_block(h + 1, s + 1, j)
                        act.wait_ge(pt_done, h * TT + (j + 1))
                        if j == 0:
                            act.wait_ge(pv_done, h + 1)
                        act.activation(pt_hi[b][:, j * T + j * P:(j + 1) * T], ps[BANK_PT + j % 2][:, j * P:T],
                                       ACT.Copy).then_inc(pt_hi_done, 1)
                    if not (isinstance(h, int) and h + 2 >= HEADS):
                        if s % 4 != 3:
                            expand(h + 2, s + 2)
                    act.wait_ge(pv_done, h + 3)
                    if s % 4 == 3 and not (isinstance(h, int) and h + 2 >= HEADS):
                        expand(h + 2, s + 2)
                    if s % 2 == 0 and not (isinstance(h, int) and h + 2 >= HEADS):
                        v_split(pair_of(h) + 1, (s // 2 + 1) % 2)
                    ro, pair = HEAD_DIM * b, pair_of(h)
                    act.activation(o_hi[ro:ro + HEAD_DIM, ts(pair, T)], ps[BANK_O + b][ro:ro + HEAD_DIM, :], ACT.Copy)\
                        .then_inc(o_hi_done, 1)

                expand(0, 0)
                expand(1, 1)
                v_split(0, 0)
                for i in range(TT):
                    exp_block(0, 0, i)
                rolled(act, HEADS, attend, last=4, unroll=4)

                def out_unit(j, s):
                    hi_split(j + (BASE["fox_out"] + 2), PAIR, (BASE["fox_out"] + s) % 2)
                    for t in range(2):
                        x_tile(n + 1, j * 2 + t, t)
                rolled(act, KD // 2, out_unit, last=2)

            def lru(n):
                def rec_unit(j, s):
                    if isinstance(j, int) and j == 0:
                        root(n)
                    hi_split(j + (BASE["rec"] + 2), PAIR, (BASE["rec"] + s) % 2)
                    for t in range(2):
                        m = j * 2 + t
                        act.wait_ge(rec_ready, m + 1)
                        act.activation(xc[:, ts(m, T)], rec_pad[t][:, 0:T], ACT.Identity,
                                       scale=par[:, bass.ds(m + COL_CONV_W, 1)],
                                       bias=par[:, bass.ds(m + COL_CONV_B, 1)]).then_inc(tap0_done, 1)
                    for t in range(2):
                        m = j * 2 + t
                        act.wait_ge(conv_step, j * 6 + (5 + t))
                        act.activation(xc_hi[:, ts(m, T)], xc[:, ts(m, T)], ACT.Copy).then_inc(xc_hi_done, 1)
                for j in range(KR // 2):
                    rec_unit(j, j % 2)
                g = 0
                for i in range(4):
                    for m0 in range(GATE_HALF):
                        m = (i // 2) * GATE_HALF + m0
                        if m0 == GATE_HALF - 1:
                            act.wait_ge(unit_done, BASE["gates"] + i + 1)
                        else:
                            act.wait_ge(gate_mm, i * (GATE_HALF - 1) + m0 + 1)
                        if i % 2 == 0:
                            act.activation(r_gate[:, ts(m, T)], ps[BANK_GATE + g % 4][:], ACT.Sigmoid,
                                           bias=col(COL_B_A, m)).then_inc(gate_out, 1)
                        else:
                            if m >= 2:
                                act.wait_ge(gi_used, m - 1)
                            act.activation(gi[m % 2][:], ps[BANK_GATE + g % 4][:], ACT.Sigmoid,
                                           bias=col(COL_B_I, m)).then_inc(gate_out, 1)
                        g += 1
                    hi_split(BASE["gates"] + i + 2, 0, (BASE["gates"] + i) % 2)
                act.wait_ge(gate_out, 4 * GATE_HALF)
                for m in range(KR):
                    act.activation(q_lru[:, ts(m, T)], r_gate[:, ts(m, T)], ACT.Tanh, scale=lru_nc[:, m:m + 1])\
                        .then_inc(tanh_done, 1)
                    act.activation(r_gate[:, ts(m, T)], r_gate[:, ts(m, T)], ACT.Exp, scale=lru_c[:, m:m + 1])\
                        .then_inc(a_done, 1)

                def gelu(m):
                    act.wait_ge(gt_ready, m + 1)
                    act.activation(gt[:, ts(m, T)], gt[:, ts(m, T)], ACT.Gelu_apprx_tanh).then_inc(gelu_done, 1)

                def y_high(m):
                    act.wait_ge(y_made, m + 1)
                    act.activation(xc_hi[:, ts(m, T)], xc[:, ts(m, T)], ACT.Copy).then_inc(y_hi_done, 1)

                for j in range(KR // 2):
                    hi_split(BASE["gate_br"] + j + 2, 0, (BASE["gate_br"] + j) % 2)
                    if j == 1:
                        for m in range(KR):
                            act.wait_ge(q_done, m + 1)
                            act.activation(q_lru[:, ts(m, T)], q_lru[:, ts(m, T)], ACT.Sqrt).then_inc(root_done, 1)
                    if j >= 2:
                        new = range(0, 6) if j == 2 else range(2 * j, 2 * j + 2)
                        for m in new:
                            gelu(m)
                        for m in new:
                            y_high(m)

                def out_tile(m, s):
                    hi_split(m + (BASE["lru_out"] + 2), COLS["lru_out"], (BASE["lru_out"] + s) % 2)
                    x_tile(n + 1, m, s)
                rolled(act, KD, out_tile, last=2)

            act.wait_ge(par_in, 16)
            act.activation(sp[:, 0:KR], par[:, COL_LAMBDA:COL_LAMBDA + KR], ACT.Abs).then_inc(lam_exp, 1)
            act.wait_ge(lam_exp, 1)
            act.activation(sp[:, KR:2 * KR], sp[:, 0:KR], ACT.Exp, scale=-1.0).then_inc(lam_exp, 1)
            hi_split(0, 0, 0)
            for m in range(KD):
                act.wait_ge(x_tile_in[m], 16)
                act.activation(xg_hi[:, ts(m, T)], x[:, ts(m, T)], ACT.Copy, scale=gain(0, m)).then_inc(xg_hi_done, 1)
                if m >= 2:
                    act.wait_ge(ssq_added, m - 1)
                act.activation(sq[:, ts(m % 2, T)], x[:, ts(m, T)], ACT.Square).then_inc(sq_done, 1)
                if m == 1:
                    hi_split(1, 0, 1)
            act.wait_ge(consts, 7)
            ffn(0, 0)
            fox(1)
            ffn(1, 2)
            ffn(2, 3)
            lru(4)
            ffn(3, 5)
            root(N_NORMS - 1)

        @block.vector
        def _(dve):
            def lo_split(u, cols, slot):
                if isinstance(u, int):
                    if u >= N_UNITS:
                        return
                    cols = UNIT_COLS[u]
                dve.wait_ge(hi_done, u + 1)
                dve.tensor_tensor(w_lo[slot][:, 0:cols], w_raw[slot][:, 0:cols], f32(w_hi[slot][:, 0:cols]),
                                  ALU.subtract).then_inc(unit_ready, 1)

            def norm_low(n, m):
                c = m + KD * n
                if n < N_NORMS - 1:
                    dve.wait_ge(xg_hi_done, c + 1)
                    dve.scalar_tensor_tensor(out=xg_lo[:, ts(m, T)], in0=x[:, ts(m, T)], scalar=gain(n, m),
                                             in1=f32(xg_hi[:, ts(m, T)]), op0=ALU.mult, op1=ALU.subtract)\
                        .then_inc(xg_ready, 1)

            def add_square(n, m, s):
                c = m + KD * n
                dve.wait_ge(sq_done, c + 1)
                dve.wait_ge(ssq_added, c) if not (isinstance(c, int) and c == 0) else None
                dve.tensor_tensor(ssq[:], ssq[:], sq[:, ts(s, T)], ALU.add).then_inc(ssq_added, 1)

            def update_x(n, m, bank, factor):
                dve.scalar_tensor_tensor(out=x[:, ts(m, T)], in0=ps[bank][:], scalar=factor, in1=x[:, ts(m, T)],
                                         op0=ALU.mult, op1=ALU.add).then_inc(x_new, 1)

            def make_r(n):
                dve.wait_ge(sqrt_done, n + 1)
                dve.reciprocal(r_bc[:], r_bc[:]).then_inc(r_ready, 1)
                if n == 1:
                    dve.wait_ge(tok_mm, 1)
                dve.memset(ssq[:], 0.0).then_inc(ssq_zero, 1)
                dve.wait_ge(r_ready, n + 1)
                dve.wait_ge(ssq_zero, n + 2)

            def ffn(f, n):
                gu_k, down_k = f"gu{f}", f"down{f}"

                def gu_unit(j, s):
                    c = j + KF * f
                    bank = 2 * ((PAIR_BASE[gu_k] + s) % 2)
                    if isinstance(j, int) and j == 0:
                        make_r(n)
                    dve.wait_ge(unit_done, j + (BASE[gu_k] + 1))
                    dve.tensor_tensor(g_buf[s][:], ps[bank][:], r_bc[:], ALU.mult).then_inc(g_ready, 1)
                    dve.tensor_tensor(u_buf[s][:], ps[bank + 1][:], r_bc[:], ALU.mult).then_inc(pair_free, 1)
                    lo_split(j + (BASE[gu_k] + 2), PAIR, (BASE[gu_k] + s) % 2)
                    dve.wait_ge(silu_done, c + 1)
                    dve.wait_ge(pair_free, j + (FREED[gu_k] + 1))
                    dve.tensor_tensor(u_buf[s][:], g_buf[s][:], u_buf[s][:], ALU.mult).then_inc(h_made, 1)
                    dve.wait_ge(h_made, c + 1)
                    dve.tensor_copy(h_hi[:, ts(j, T)], u_buf[s][:]).then_inc(h_hi_done, 1)
                    dve.wait_ge(h_hi_done, c + 1)
                    dve.tensor_tensor(h_lo[:, ts(j, T)], u_buf[s][:], f32(h_hi[:, ts(j, T)]), ALU.subtract)\
                        .then_inc(h_ready, 1)
                rolled(dve, KF, gu_unit, first=2, last=2)

                def down_tile(m, s):
                    u = m * 2 + (BASE[down_k] + 2)
                    lo_split(u, DOWN, BASE[down_k] % 2)
                    dve.wait_ge(unit_done, u)
                    update_x(n + 1, m, BANK_DOWN + s, 0.5)
                    norm_low(n + 1, m)
                    add_square(n + 1, m, s)
                    lo_split(u + 1, DOWN, (BASE[down_k] + 1) % 2)
                rolled(dve, KD, down_tile, last=2)

            def fox(n):
                def qk_unit(j, s):
                    bank = 2 * ((PAIR_BASE["qk"] + s) % 2)
                    if isinstance(j, int) and j == 0:
                        make_r(n)
                        dve.wait_ge(tok_sqrt, 1)
                        dve.reciprocal(r_tok[:], r_tok[:]).then_inc(tok_ready, 1)
                    dve.wait_ge(unit_done, j + (BASE["qk"] + 1))
                    dve.tensor_tensor(q_raw[:, ts(j, T)], ps[bank][:], r_bc[:], ALU.mult)
                    dve.tensor_tensor(k_raw[:, ts(j, T)], ps[bank + 1][:], r_bc[:], ALU.mult).then_inc(pair_free, 1)
                    lo_split(j + (BASE["qk"] + 2), PAIR, (BASE["qk"] + s) % 2)
                rolled(dve, KD, qk_unit, first=2, last=2)

                dve.wait_ge(unit_done, BASE["f"] + 1)
                hp = slice(0, HEADS)
                dve.tensor_tensor(fl_a[:], ps[BANK_F][hp, :], r_bc[hp, :], ALU.mult).then_inc(f_step, 1)
                dve.wait_ge(f_step, 1)
                dve.tensor_scalar(fl_a[:], fl_a[:], par[hp, COL_B_F:COL_B_F + 1], None, ALU.add).then_inc(f_step, 1)
                lo_split(BASE["f"] + 2, 0, BASE["f"] % 2)
                dve.memset(f32(one_zero[:, 0:T]), 1.0).then_inc(f_step, 1)
                dve.memset(f32(one_zero[:, T:2 * T]), 0.0).then_inc(f_step, 1)
                dve.memset(fl_c[:], 1.0).then_inc(f_step, 1)
                dve.wait_ge(f_exp, 3)
                dve.scalar_tensor_tensor(out=fl_a[:], in0=fl_a[:], scalar=0.0, in1=fl_b[:], op0=ALU.min,
                                         op1=ALU.subtract).then_inc(f_step, 1)
                dve.wait_ge(f_step, 6)
                dve.tensor_tensor_scan(fl_b[:], fl_c[:], fl_a[:], 0.0, ALU.mult, ALU.add).then_inc(f_step, 1)
                dve.wait_ge(f_step, 7)
                dve.tensor_copy(f_pack[:, 0:T], fl_b[:]).then_inc(f_step, 1)
                dve.wait_ge(f_step, 8)
                dve.tensor_tensor(f_pack[:, T:2 * T], fl_b[:], f32(f_pack[:, 0:T]), ALU.subtract).then_inc(f_step, 1)
                dve.wait_ge(f_step, 9)
                dve.tensor_scalar(f_pack[:, 2 * T:4 * T], f32(f_pack[:, 0:2 * T]), -1.0, None, ALU.mult)\
                    .then_inc(f_packed, 1)
                for i in range(4):
                    lo_split(BASE["v"] + i + 2, 0, (BASE["v"] + i) % 2)

                def expand(h, s):
                    b, ro, pair = s % 2, HEAD_DIM * (s % 2), pair_of(h)
                    dve.wait_ge(*((pair_free, FREED["qk"] + KD) if isinstance(h, int) and h == 0 else (head_ready, h)))
                    dve.tensor_copy(head_tmp[0:HEAD_DIM, T:2 * T], k_raw[ro:ro + HEAD_DIM, ts(pair, T)])\
                        .then_inc(k_tmp, 1)
                    dve.wait_ge(head_hi, h + 1)
                    dve.tensor_tensor(head[b][0:HEAD_DIM, 2 * T:4 * T], head_tmp[0:HEAD_DIM, :],
                                      f32(head[b][0:HEAD_DIM, 0:2 * T]), ALU.subtract).then_inc(head_ready, 1)

                def v_split(pair, vb):
                    dve.wait_ge(v_hi_done, pair + 1)
                    src = v_raw[:].rearrange("p (t n) -> p t n", t=TT)[:, :, ts(pair, P)]
                    dve.tensor_tensor(v_lo[vb][:].rearrange("p (t n) -> p t n", t=TT), src,
                                      f32(v_hi[vb][:]).rearrange("p (t n) -> p t n", t=TT), ALU.subtract)\
                        .then_inc(v_ready, 1)

                def max_block(h, s, i):
                    b = s % 2
                    dve.wait_ge(scores_done, h * TT + (i + 1))
                    dve.tensor_reduce(neg_max[:, b * TT + i:b * TT + i + 1], ps[i][:, 0:(i + 1) * P], AX.X, ALU.max,
                                      negate=True).then_inc(max_done, 1)

                def normalise(h, s):
                    b = s % 2
                    dve.wait_ge(exp_done, (h + 1) * TT)
                    dve.reciprocal(row_rcp[:, ts(b, TT)], row_sum[:, ts(b, TT)]).then_inc(rcp_done, 1)
                    dve.wait_ge(rcp_done, h + 1)
                    for i in range(TT):
                        w, at_ = (i + 1) * P, P * (i * (i + 1) // 2)
                        dve.tensor_scalar(prob[b][:, at_:at_ + w], prob[b][:, at_:at_ + w],
                                          row_rcp[:, b * TT + i:b * TT + i + 1], None, ALU.mult).then_inc(prob_ready, 1)

                def attend(h, s):
                    more = not (isinstance(h, int) and h == HEADS - 1)
                    b = s % 2
                    for j in range(TT):
                        if more:
                            max_block(h + 1, s + 1, j)
                        dve.wait_ge(pt_hi_done, h * TT + (j + 1))
                        kk = slice(j * T + j * P, (j + 1) * T)
                        dve.tensor_tensor(pt_lo[b][:, kk], ps[BANK_PT + j % 2][:, j * P:T], f32(pt_hi[b][:, kk]),
                                          ALU.subtract).then_inc(pt_ready, 1)
                    if more:
                        normalise(h + 1, s + 1)
                    if not (isinstance(h, int) and h + 2 >= HEADS):
                        expand(h + 2, s + 2)
                        if s % 2 == 0:
                            v_split(pair_of(h) + 1, (s // 2 + 1) % 2)
                    ro, pair = HEAD_DIM * b, pair_of(h)
                    dve.wait_ge(o_hi_done, h + 1)
                    dve.tensor_tensor(o_lo[ro:ro + HEAD_DIM, ts(pair, T)], ps[BANK_O + b][ro:ro + HEAD_DIM, :],
                                      f32(o_hi[ro:ro + HEAD_DIM, ts(pair, T)]), ALU.subtract).then_inc(o_ready, 1)

                expand(0, 0)
                expand(1, 1)
                v_split(0, 0)
                for i in range(TT):
                    max_block(0, 0, i)
                normalise(0, 0)
                rolled(dve, HEADS, attend, last=4, unroll=4)

                def out_unit(j, s):
                    bank = 2 * ((PAIR_BASE["fox_out"] + s) % 2)
                    dve.wait_ge(unit_done, j + (BASE["fox_out"] + 1))
                    for t in range(2):
                        update_x(n + 1, j * 2 + t, bank + t, 1.0)
                    norm_low(n + 1, j * 2)
                    dve.wait_ge(xg_hi_done, j * 2 + (KD * (n + 1) + 2))
                    m = j * 2 + 1
                    dve.scalar_tensor_tensor(out=xg_lo[:, ts(m, T)], in0=x[:, ts(m, T)], scalar=gain(n + 1, m),
                                             in1=f32(xg_hi[:, ts(m, T)]), op0=ALU.mult, op1=ALU.subtract)\
                        .then_inc(xg_ready, 1)
                    add_square(n + 1, j * 2, 0)
                    add_square(n + 1, m, 1)
                    lo_split(j + (BASE["fox_out"] + 2), PAIR, (BASE["fox_out"] + s) % 2)
                rolled(dve, KD // 2, out_unit, last=2)

            def lru(n):
                dve.memset(rec_pad[0][:, 0:TAPS - 1], 0.0)
                dve.memset(rec_pad[1][:, 0:TAPS - 1], 0.0)

                def rec_unit(j, s):
                    bank = 2 * ((PAIR_BASE["rec"] + s) % 2)
                    if isinstance(j, int) and j == 0:
                        make_r(n)
                    dve.wait_ge(unit_done, j + (BASE["rec"] + 1))
                    for t in range(2):
                        dve.tensor_tensor(rec_pad[t][:, TAPS - 1:TAPS - 1 + T], ps[bank + t][:], r_bc[:], ALU.mult)\
                            .then_inc(rec_ready, 1)
                    lo_split(j + (BASE["rec"] + 2), PAIR, (BASE["rec"] + s) % 2)
                    for tap in range(1, TAPS):
                        for t in range(2):
                            m = j * 2 + t
                            if tap == 1:
                                dve.wait_ge(tap0_done, m + 1)
                            else:
                                dve.wait_ge(conv_step, conv_count(j, tap - 1, t))
                            xm = xc[:, ts(m, T)]
                            dve.scalar_tensor_tensor(out=xm, in0=rec_pad[t][:, tap:tap + T],
                                                     scalar=par[:, bass.ds(m + (COL_CONV_W + tap * KR), 1)],
                                                     in1=xm, op0=ALU.mult, op1=ALU.add).then_inc(conv_step, 1)
                    for t in range(2):
                        m = j * 2 + t
                        dve.wait_ge(xc_hi_done, m + 1)
                        dve.tensor_tensor(xc_lo[:, ts(m, T)], xc[:, ts(m, T)], f32(xc_hi[:, ts(m, T)]), ALU.subtract)\
                            .then_inc(xc_ready, 1)

                def conv_count(j, tap, t):
                    return j * 6 + (2 * (tap - 1) + t + 1)

                for j in range(KR // 2):
                    rec_unit(j, j % 2)
                g = 0
                for i in range(4):
                    for m0 in range(GATE_HALF):
                        m = (i // 2) * GATE_HALF + m0
                        g += 1
                        if i % 2 == 1:
                            dve.wait_ge(gate_out, g)
                            dve.tensor_tensor(xc[:, ts(m, T)], gi[m % 2][:], xc[:, ts(m, T)], ALU.mult).then_inc(gi_used, 1)
                    lo_split(BASE["gates"] + i + 2, 0, (BASE["gates"] + i) % 2)

                def one_minus_a2(m):
                    qm = q_lru[:, ts(m, T)]
                    dve.wait_ge(tanh_done, m + 1)
                    if m:
                        dve.wait_ge(q_done, m)
                    dve.tensor_scalar(den[:], qm, 1.0, None, ALU.add).then_inc(q_step, 1)
                    dve.wait_ge(q_step, 2 * m + 1)
                    dve.reciprocal(den[:], den[:]).then_inc(q_step, 1)
                    dve.wait_ge(q_step, 2 * m + 2)
                    dve.scalar_tensor_tensor(out=qm, in0=qm, scalar=2.0, in1=den[:], op0=ALU.mult, op1=ALU.mult)\
                        .then_inc(q_done, 1)

                def recur(m):
                    xm, qm = xc[:, ts(m, T)], q_lru[:, ts(m, T)]
                    dve.wait_ge(root_done, m + 1)
                    dve.tensor_tensor(xm, qm, xm, ALU.mult).then_inc(b_done, 1)
                    dve.wait_ge(b_done, m + 1)
                    dve.wait_ge(a_done, m + 1)
                    dve.tensor_tensor_scan(qm, r_gate[:, ts(m, T)], xm, 0.0, ALU.mult, ALU.add).then_inc(scan_done, 1)

                def gated(m):
                    dve.wait_ge(scan_done, m + 1)
                    dve.wait_ge(gelu_done, m + 1)
                    dve.tensor_tensor(xc[:, ts(m, T)], q_lru[:, ts(m, T)], gt[:, ts(m, T)], ALU.mult).then_inc(y_made, 1)

                def y_low(m):
                    dve.wait_ge(y_hi_done, m + 1)
                    dve.tensor_tensor(xc_lo[:, ts(m, T)], xc[:, ts(m, T)], f32(xc_hi[:, ts(m, T)]), ALU.subtract)\
                        .then_inc(y_ready, 1)

                for m in range(0, 4):
                    one_minus_a2(m)
                for j in range(KR // 2):
                    bank = 2 * ((PAIR_BASE["gate_br"] + j) % 2)
                    dve.wait_ge(unit_done, BASE["gate_br"] + j + 1)
                    for t in range(2):
                        dve.tensor_tensor(gt[:, ts(2 * j + t, T)], ps[bank + t][:], r_bc[:], ALU.mult).then_inc(gt_ready, 1)
                    lo_split(BASE["gate_br"] + j + 2, 0, (BASE["gate_br"] + j) % 2)
                    if j < 2:
                        for m in range(4 + 3 * j, 7 + 3 * j):
                            one_minus_a2(m)
                    if j == 2:
                        for m in range(0, 6):
                            recur(m)
                    if j == 3:
                        for m in range(6, KR):
                            recur(m)
                    if j >= 2:
                        new = range(0, 6) if j == 2 else range(2 * j, 2 * j + 2)
                        for m in new:
                            gated(m)
                        for m in new:
                            y_low(m)

                def out_tile(m, s):
                    dve.wait_ge(unit_done, m + (BASE["lru_out"] + 1))
                    update_x(n + 1, m, BANK_DOWN + s, 1.0)
                    norm_low(n + 1, m)
                    add_square(n + 1, m, s)
                    lo_split(m + (BASE["lru_out"] + 2), COLS["lru_out"], (BASE["lru_out"] + s) % 2)
                rolled(dve, KD, out_tile, last=2)

            dve.memset(ssq[:], 0.0).then_inc(ssq_zero, 1)
            dve.wait_ge(par_in, 16)
            lam = par[:, COL_LAMBDA:COL_LAMBDA + KR]
            dve.wait_ge(ssq_zero, 1)
            lo_split(0, 0, 0)
            for m in range(KD):
                norm_low(0, m)
                add_square(0, m, m % 2)
                if m == 1:
                    lo_split(1, 0, 1)

            e, s_, s2, pl = (sp[:, ts(i, KR)] for i in (1, 2, 3, 4))
            n_step = [0]

            def step(ins):
                n_step[0] += 1
                ins.then_inc(lam_step, 1)
                dve.wait_ge(lam_step, n_step[0])
            dve.wait_ge(lam_exp, 2)
            step(dve.tensor_scalar(s_, e, 2.0, None, ALU.add))
            step(dve.reciprocal(s_, s_))
            step(dve.tensor_tensor(s_, e, s_, ALU.mult))
            step(dve.tensor_tensor(s2, s_, s_, ALU.mult))
            step(dve.tensor_scalar(pl, s2, 1.0 / 17, None, ALU.mult))
            for k in (15, 13, 11, 9, 7, 5, 3):
                step(dve.scalar_tensor_tensor(out=pl, in0=pl, scalar=1.0 / k, in1=s2, op0=ALU.add, op1=ALU.mult))
            step(dve.scalar_tensor_tensor(out=pl, in0=pl, scalar=1.0, in1=s_, op0=ALU.add, op1=ALU.mult))
            step(dve.tensor_scalar(s2, lam, -1.0, 0.0, ALU.mult, ALU.max))
            step(dve.scalar_tensor_tensor(out=pl, in0=pl, scalar=2.0, in1=s2, op0=ALU.mult, op1=ALU.add))
            step(dve.tensor_scalar(lru_c[:], pl, -RG_C, None, ALU.mult))
            step(dve.tensor_scalar(lru_nc[:], pl, RG_C, None, ALU.mult))
            ffn(0, 0)
            fox(1)
            ffn(1, 2)
            ffn(2, 3)
            lru(4)
            ffn(3, 5)
            make_r(N_NORMS - 1)
            for m in range(KD):
                dve.scalar_tensor_tensor(out=x[:, ts(m, T)], in0=x[:, ts(m, T)], scalar=gain(N_NORMS - 1, m),
                                         in1=r_bc[:], op0=ALU.mult, op1=ALU.mult).then_inc(out_made, 1)


def lay_out(a):
    def pairs(w, groups, n):
        if groups == 2:
            return w.reshape(KD, P, 2, n, P).transpose(3, 1, 0, 2, 4).reshape(n, P, PAIR)
        return w.reshape(KD, P, n, 2, P).transpose(2, 1, 0, 3, 4).reshape(n, P, PAIR)

    def interleave(w1, w2):
        return [w[i] for i in range(DEPTH) for w in (w1, w2)]

    cols = []
    norms = [g for i in range(DEPTH) for g in (a["ffn1_norm"][i], a["mix_norm"][i], a["ffn2_norm"][i])]
    for g in norms + [a["final_norm"]]:
        cols.append(g.reshape(KD, P).T)
    cols += [a["lru_conv_w"][0, j].reshape(KR, P).T for j in range(TAPS)]
    cols += [a[k][0].reshape(KR, P).T for k in ("lru_conv_b", "lru_b_a", "lru_b_i", "lru_lambda")]
    b_f = np.zeros((P, 1), np.float32)
    b_f[:HEADS, 0] = a["fox_b_f"][0]
    params = np.concatenate(cols + [b_f], 1)

    w_in = a["fox_w_in"][0]
    f_w = np.zeros((KD, P, P), np.float32)
    f_w[:, :, :HEADS] = w_in[:, 3 * D:].reshape(KD, P, HEADS)
    gates = []
    dense = []
    for w in (a["lru_w_a"][0], a["lru_w_i"][0]):
        full = np.zeros((R, R), np.float32)
        for b in range(LRU_BLOCKS):
            at = slice(b * LRU_BLOCK, (b + 1) * LRU_BLOCK)
            full[at, at] = w[b]
        dense.append(full)
    for half in range(2):
        for full in dense:
            gates.append(np.concatenate([full[k * P:(k + 1) * P, m * P:(m + 1) * P]
                                         for m in range(half * GATE_HALF, (half + 1) * GATE_HALF) for k in BAND[m]], 1))
    lru_in = a["lru_w_in"][0]
    return {
        "x_t": a["x"][0].T.reshape(KD, P, T),
        "params": params,
        "gu": np.stack([pairs(w, 2, KF) for w in interleave(a["ffn1_w_gu"], a["ffn2_w_gu"])]),
        "down": np.stack([w.reshape(2, HALF_F, P, KD, P).transpose(3, 0, 2, 1, 4).reshape(2 * KD, P, DOWN)
                          for w in interleave(a["ffn1_w_down"], a["ffn2_w_down"])]),
        "qk": pairs(w_in[:, :2 * D], 2, KD),
        "f_w": f_w.transpose(1, 0, 2).reshape(1, P, KD * P),
        "v_w": w_in[:, 2 * D:3 * D].reshape(2, KD // 2, P, 2, T).transpose(3, 0, 2, 1, 4).reshape(4, P, PAIR),
        "fox_out": pairs(a["fox_w_out"][0], 1, KD // 2),
        "rec": pairs(lru_in[:, R:], 1, KR // 2),
        "gates": np.stack(gates),
        "gate_br": pairs(lru_in[:, :R], 1, KR // 2),
        "lru_out": a["lru_w_out"][0].reshape(KR, P, KD, P).transpose(2, 1, 0, 3).reshape(KD, P, KR * P),
    }


def kernel(**inputs):
    import concourse.bacc as _bacc
    from concourse.bass_utils import run_bass_kernel_spmd as _run

    nc = _bacc.Bacc("TRN2", target_bir_lowering=False, num_devices=1)
    arrays, args = {}, []
    for name, a in lay_out({k: np.asarray(v) for k, v in inputs.items()}).items():
        a = np.ascontiguousarray(a)
        arrays[f"in_{name}_dram"] = a
        args.append(nc.dram_tensor(f"in_{name}_dram", a.shape, mybir.dt.from_np(a.dtype), kind="ExternalInput").ap())
    args.append(nc.dram_tensor("out_dram", (KD, P, T), F32, kind="ExternalOutput").ap())
    build_trunk(nc, *args)
    r = _run(nc, [arrays], core_ids=[0])
    return np.ascontiguousarray(r.results[0]["out_dram"].reshape(D, T).T)[None]
```

```python
from contextlib import ExitStack

import numpy as np

import concourse.bass as bass
from concourse import mybir

F32 = mybir.dt.float32
F32R = mybir.dt.float32r
ALU = mybir.AluOpType
ACT = mybir.ActivationFunctionType
AX = mybir.AxisListType
ts = bass.ts

P = 128
T = 512
D = 1024
DEPTH = 2
HEADS = 16
HEAD_DIM = D // HEADS
R = (4 * D // 3) // 128 * 128
LRU_BLOCKS = 16
LRU_BLOCK = R // LRU_BLOCKS
TAPS = 4
RG_C = 8.0
D_FF = (8 * D // 3 + 255) // 256 * 256
EPS = 1e-6

KD = D // P
KF = D_FF // P
KR = R // P
TT = T // P
HALF_F = KF // 2
N_FFN = 2 * DEPTH
N_NORMS = 3 * DEPTH + 1
MASKED = -1e30

GATE_HALF = 5
BAND = [[i for i in range(KR)
         if any(b * LRU_BLOCK < (m + 1) * P and (b + 1) * LRU_BLOCK > m * P
                and b * LRU_BLOCK < (i + 1) * P and (b + 1) * LRU_BLOCK > i * P
                for b in range(LRU_BLOCKS))] for m in range(KR)]
GATE_BLOCKS = sum(len(BAND[m]) for m in range(GATE_HALF))

COL_GAIN = 0
COL_CONV_W = COL_GAIN + N_NORMS * KD
COL_CONV_B = COL_CONV_W + TAPS * KR
COL_B_A = COL_CONV_B + KR
COL_B_I = COL_B_A + KR
COL_LAMBDA = COL_B_I + KR
COL_B_F = COL_LAMBDA + KR
N_PARAMS = COL_B_F + 1

PAIR = 2 * KD * P
DOWN = HALF_F * P
STREAM = [
    ("gu0", KF, PAIR), ("down0", 2 * KD, DOWN),
    ("qk", KD, PAIR), ("f", 1, KD * P), ("v", 4, PAIR), ("fox_out", KD // 2, PAIR),
    ("gu1", KF, PAIR), ("down1", 2 * KD, DOWN),
    ("gu2", KF, PAIR), ("down2", 2 * KD, DOWN),
    ("rec", KR // 2, PAIR), ("gates", 4, GATE_BLOCKS * P), ("gate_br", KR // 2, PAIR),
    ("lru_out", KD, KR * P),
    ("gu3", KF, PAIR), ("down3", 2 * KD, DOWN),
]
BASE, COLS, UNIT_COLS = {}, {}, []
for _kind, _n, _cols in STREAM:
    BASE[_kind], COLS[_kind] = len(UNIT_COLS), _cols
    UNIT_COLS += [_cols] * _n
N_UNITS = len(UNIT_COLS)

PAIR_BASE, _q = {}, 0
for _kind, _n, _cols in STREAM:
    if _kind in ("qk", "fox_out", "rec", "gate_br") or _kind.startswith("gu"):
        PAIR_BASE[_kind] = _q
        _q += _n
FREED = {"gu0": 0, "qk": KF, "gu1": KF + KD, "gu2": 2 * KF + KD, "gu3": 3 * KF + KD}


def build_trunk(nc, x_t, params, gu, down, qk, f_w, v_w, fox_out, rec, gates, gate_br, lru_out, out_t):
    ctx = ExitStack()
    with ctx:
        base = (nc.sbuf_base + 31) // 32 * 32
        nc_room = nc.sbuf_bytes_remaining
        ctx.enter_context(nc.sbuf_tensor("slab", [P, (nc.sbuf_bytes_remaining - 64) // 4], F32))
        end = [0]

        def place(at, name, cols, dt=F32, parts=P):
            return nc.alloc_sbuf_tensor_at(name, [parts, cols], dt, offset=base + 4 * at)

        def area(cols):
            at = end[0]
            end[0] = at + (cols + 7) // 8 * 8
            return at

        def sb(name, cols, dt=F32, parts=P):
            return place(area(cols), name, cols, dt, parts)

        def sem(name):
            return ctx.enter_context(nc.semaphore(name))

        x = sb("x", KD * T)
        w_raw = [sb(f"w_raw{i}", PAIR) for i in range(2)]
        w_hi = [sb(f"w_hi{i}", PAIR, F32R) for i in range(2)]
        w_lo = [sb(f"w_lo{i}", PAIR, F32R) for i in range(2)]
        par = sb("par", N_PARAMS)
        r_bc = sb("r_bc", T)
        ssq = sb("ssq", T)
        sq_at = area(2 * T)
        sq = place(sq_at, "sq", 2 * T)
        ones = sb("ones", P)
        ident = sb("ident", P)
        ident_r = sb("ident_r", P, F32R)
        mask_r = sb("mask_r", P, F32R)
        eps = sb("eps", 1)
        r_tok = sb("r_tok", TT)
        lru_c = sb("lru_c", KR)
        lru_nc = sb("lru_nc", KR)
        sp = sb("sp", 6 * KR)
        neg_max = sb("neg_max", TT)
        row_sum = sb("row_sum", TT)
        row_rcp = sb("row_rcp", TT)

        xg_area = area(2 * KD * T)
        h_area = area(2 * KF * T)
        t_area = area(4 * T)
        assert 4 * end[0] + 64 <= nc_room, (4 * end[0], nc_room)

        xg_hi = place(xg_area, "xg_hi", KD * T, F32R)
        xg_lo = place(xg_area + KD * T, "xg_lo", KD * T, F32R)
        h_hi = place(h_area, "h_hi", KF * T, F32R)
        h_lo = place(h_area + KF * T, "h_lo", KF * T, F32R)
        g_buf = [place(t_area + i * T, f"g_buf{i}", T) for i in range(2)]
        u_buf = [place(t_area + (2 + i) * T, f"u_buf{i}", T) for i in range(2)]
        q_raw = place(h_area, "q_raw", KD * T)
        k_raw = place(h_area + KD * T, "k_raw", KD * T)
        o_hi = place(h_area, "o_hi", KD * T, F32R)
        o_lo = place(h_area + KD * T, "o_lo", KD * T, F32R)
        at = 2 * KD * T
        v_raw = place(h_area + at, "v_raw", TT * D)
        at += TT * D
        forget = [place(h_area + at + i * 2 * T, f"forget{i}", 2 * T, F32R) for i in range(2)]
        at += 4 * T
        QK_COLS, V_COLS, BLOCK_COLS = 6 * T, 2 * TT * P, P * TT * (TT + 1) // 2
        qk_at = [h_area + at, xg_area]
        at += QK_COLS
        v_at = [h_area + at, xg_area + QK_COLS]
        at += 2 * V_COLS
        prob = place(h_area + at, "prob", BLOCK_COLS)
        at += BLOCK_COLS
        assert at <= 2 * KF * T
        qk_split = [place(qk_at[i], f"qk_split{i}", QK_COLS, F32R) for i in range(2)]
        v_hi = [place(v_at[i], f"v_hi{i}", V_COLS, F32R) for i in range(2)]
        v_lo = [place(v_at[i] + V_COLS, f"v_lo{i}", V_COLS, F32R) for i in range(2)]
        pt_at = xg_area + QK_COLS + 2 * V_COLS
        PT_COLS = (2 + TT) * 2 * P
        pt_hi = place(pt_at, "pt_hi", PT_COLS, F32R)
        pt_lo = place(pt_at + PT_COLS, "pt_lo", PT_COLS, F32R)
        assert pt_at + 2 * PT_COLS <= xg_area + 2 * KD * T
        f_pack = place(t_area, "f_pack", 2 * T, F32R, 32 + HEADS)
        fl_a, fl_b, fl_c = (place(qk_at[0] + i * T, f"fl_{'abc'[i]}", T, F32, HEADS) for i in range(3))
        r_gate = place(h_area, "r_gate", KR * T)
        xc = place(h_area + KR * T, "xc", KR * T)
        xc_hi = place(h_area + 2 * KR * T, "xc_hi", KR * T, F32R)
        xc_lo = place(h_area + 3 * KR * T, "xc_lo", KR * T, F32R)
        q_lru = place(h_area + 2 * KR * T, "q_lru", KR * T)
        gt = place(h_area + 3 * KR * T, "gt", KR * T)
        rec_pad = [place(t_area + i * (T + 8), f"rec_pad{i}", T + TAPS - 1) for i in range(2)]
        den = place(t_area + 2 * (T + 8), "den", T)
        gi = [place(sq_at + i * T, f"gi{i}", T) for i in range(2)]

        ps = [ctx.enter_context(nc.psum_tensor(f"ps{b}", [P, T], F32)) for b in range(8)]
        BANK_DOWN, BANK_SSQ, BANK_TOK, BANK_F = 4, 6, 7, 5
        BANK_PT, BANK_O, BANK_GATE, BANK_V = 4, 6, 4, 4

        par_in = sem("par_in")
        x_tile_in = [sem(f"x_tile_in{k}") for k in range(KD)]
        raw_in = [sem(f"raw_in{i}") for i in range(2)]
        hi_done = sem("hi_done")
        unit_ready = sem("unit_ready")
        unit_done = sem("unit_done")
        pair_free = sem("pair_free")
        x_new = sem("x_new")
        xg_hi_done = sem("xg_hi_done")
        xg_ready = sem("xg_ready")
        sq_done = sem("sq_done")
        ssq_added = sem("ssq_added")
        ssq_mm = sem("ssq_mm")
        sqrt_done = sem("sqrt_done")
        r_ready = sem("r_ready")
        ssq_zero = sem("ssq_zero")
        consts = sem("consts")
        g_ready = sem("g_ready")
        silu_done = sem("silu_done")
        h_made = sem("h_made")
        h_hi_done = sem("h_hi_done")
        h_ready = sem("h_ready")
        tok_mm = sem("tok_mm")
        tok_sqrt = sem("tok_sqrt")
        tok_ready = sem("tok_ready")
        f_step = sem("f_step")
        f_exp = sem("f_exp")
        f_packed = sem("f_packed")
        rows_in = [sem(f"rows_in{i}") for i in range(2)]
        v_raw_done = sem("v_raw_done")
        pads = sem("pads")
        qk_hi_done = sem("qk_hi_done")
        qk_ready = sem("qk_ready")
        v_hi_done = sem("v_hi_done")
        v_ready = sem("v_ready")
        scores_done = sem("scores_done")
        max_done = sem("max_done")
        exp_done = sem("exp_done")
        rcp_done = sem("rcp_done")
        prob_ready = sem("prob_ready")
        pt_done = sem("pt_done")
        pt_hi_done = sem("pt_hi_done")
        pt_ready = sem("pt_ready")
        pv_done = sem("pv_done")
        o_hi_done = sem("o_hi_done")
        o_ready = sem("o_ready")
        lam_exp = sem("lam_exp")
        lam_step = sem("lam_step")
        rec_ready = sem("rec_ready")
        conv_step = sem("conv_step")
        tap0_done = sem("tap0_done")
        xc_hi_done = sem("xc_hi_done")
        xc_ready = sem("xc_ready")
        gate_mm = sem("gate_mm")
        gate_out = sem("gate_out")
        gi_used = sem("gi_used")
        tanh_done = sem("tanh_done")
        a_done = sem("a_done")
        q_step = sem("q_step")
        q_done = sem("q_done")
        root_done = sem("root_done")
        b_done = sem("b_done")
        scan_done = sem("scan_done")
        gt_ready = sem("gt_ready")
        gelu_done = sem("gelu_done")
        y_made = sem("y_made")
        y_hi_done = sem("y_hi_done")
        y_ready = sem("y_ready")
        out_made = sem("out_made")
        out_in_dram = sem("out_in_dram")

        def gain(n, m):
            return par[:, bass.ds(m + (COL_GAIN + n * KD), 1)]

        def col(base, m):
            return par[:, base + m:base + m + 1]

        def f32(ap):
            return ap.bitcast(F32)

        def rolled(eng, n, body, first=0, last=0, unroll=2):
            for k in range(first):
                body(k, k % unroll)
            turns = (n - first - last) // unroll
            if turns > 0:
                with eng.Fori(0, turns) as i:
                    for s in range(unroll):
                        body(i * unroll + (first + s), (first + s) % unroll)
            for k in range(first + max(turns, 0) * unroll, n):
                body(k, k % unroll)

        def pair_of(h):
            return h // 2

        def v_of_pair(pair):
            return v_raw[:].rearrange("p (t c n) -> p t c n", t=TT, n=HEAD_DIM)[:, :, bass.ds(pair * 2, 2), :]

        def v_view(ap):
            return ap.rearrange("p (t c n) -> p t c n", t=TT, n=HEAD_DIM)[:, :, 0:4:3, :]

        def pt_block(buf, i):
            at_ = (i // 2) * 4 * P
            return buf[:, at_:at_ + (i + 1) * 2 * P].rearrange("p (j n) -> p j n", j=i + 1)[:, :, (i % 2) * P:(i % 2 + 1) * P]

        def ahead(step, h, s, i):
            if not (isinstance(h, int) and h + i // TT >= HEADS):
                step(h + i // TT, s + i // TT, i % TT)

        block = ctx.enter_context(nc.Block())

        @block.sync
        def _(sp_):
            sp_.dma_start(par[:], params).then_inc(par_in, 16)
            for k in range(KD // 2):
                sp_.dma_start(x[:, ts(k, T)], x_t[k]).then_inc(x_tile_in[k], 16)

            def load(dram, base, cols):
                def body(k, s):
                    u = k + base
                    slot = (base + s) % 2
                    if not (isinstance(u, int) and u < 2):
                        sp_.wait_ge(unit_ready, u - 1)
                    sp_.dma_start(w_raw[slot][:, 0:cols],
                                  dram[bass.ds(k, 1)].rearrange("a p n -> (a p) n")).then_inc(raw_in[slot], 16)
                return body

            for kind, n, cols in STREAM:
                dram = {"qk": qk, "f": f_w, "v": v_w, "fox_out": fox_out, "rec": rec, "gates": gates,
                        "gate_br": gate_br, "lru_out": lru_out}.get(kind)
                if dram is None:
                    dram = (gu if kind.startswith("gu") else down)[int(kind[-1])]
                rolled(sp_, n, load(dram, BASE[kind], cols), first=2 if kind == "gu0" else 0)

            for m in range(KD):
                sp_.wait_ge(out_made, m + 1)
                sp_.dma_start(out_t[m], x[:, ts(m, T)]).then_inc(out_in_dram, 16)
            sp_.wait_ge(out_in_dram, 16 * KD)

        @block.gpsimd
        def _(pool):
            pool.memset(eps[:], EPS).then_inc(consts, 1)
            pool.memset(ones[:], 1.0).then_inc(consts, 1)
            pool.memset(ident[:], 1.0).then_inc(consts, 1)
            pool.memset(f32(mask_r[:]), 0.0).then_inc(consts, 1)
            pool.wait_ge(consts, 4)
            pool.affine_select(out=ident[:], in_=ident[:], compare_op=ALU.is_equal, fill=0.0, base=0,
                               pattern=[[-1, P]], channel_multiplier=1).then_inc(consts, 1)
            pool.affine_select(out=mask_r[:], in_=f32(mask_r[:]), compare_op=ALU.is_ge, fill=MASKED, base=0,
                               pattern=[[-1, P]], channel_multiplier=1).then_inc(consts, 1)
            pool.wait_ge(consts, 6)
            pool.tensor_copy(ident_r[:], ident[:]).then_inc(consts, 1)
            pool.sem_inc(pt_ready, 2)
            pool.sem_inc(o_ready, 2)

            n_pads = [0]

            def pad(ap, value):
                if n_pads[0]:
                    pool.wait_ge(pads, n_pads[0])
                pool.memset(f32(ap), value).then_inc(pads, 1)
                n_pads[0] += 1

            def pad_q(i):
                pad(qk_split[i][HEAD_DIM:P, 0:2 * T], 0.0)
                pad(qk_split[i][0:HEAD_DIM, 2 * T:4 * T], 0.0)

            def pad_v(i):
                pad(v_hi[i][:], 0.0)
                pad(v_lo[i][:], 0.0)

            pool.wait_ge(unit_done, BASE["qk"])
            for i in range(2):
                pad(forget[i][:], 0.0)
                pad(forget[i][32:34, 0:T], 1.0)
                pad(forget[i][0:2, T:2 * T], 1.0)
            pad_v(0)
            pool.wait_ge(pads, 8)
            pool.wait_ge(f_packed, 2)
            pad_q(0)

            def rows(h):
                b = h % 2
                if h >= 2:
                    pool.wait_ge(scores_done, (h - 1) * TT)
                for row, cols in ((0, slice(0, T)), (32, slice(T, 2 * T))):
                    pool.dma_start(forget[b][row:row + 2, cols], f_pack[h:h + 33:32, cols]).then_inc(rows_in[b], 16)

            rows(0)
            rows(1)
            pool.wait_ge(unit_done, BASE["fox_out"])
            pad_q(1)
            pad_v(1)
            for h in range(2, HEADS):
                rows(h)

        @block.tensor
        def _(pe):
            def mm3(dst, a_hi, a_lo, b_hi, b_lo, start, stop):
                pe.matmul(dst, a_hi, b_hi, start=start, stop=False)
                pe.matmul(dst, a_hi, b_lo, start=False, stop=False)
                return pe.matmul(dst, a_lo, b_hi, start=False, stop=stop)

            def sum_squares(n):
                pe.wait_ge(ssq_added, KD * (n + 1))
                pe.matmul(ps[BANK_SSQ][:], ones[:], ssq[:], start=True, stop=True).then_inc(ssq_mm, 1)

            def pair_unit(base, pair_base, src_hi, src_lo, bank_free, ready=None, after_first=None):
                def body(j, s):
                    u = j + base
                    slot, bank = (base + s) % 2, 2 * ((pair_base + s) % 2)
                    first = isinstance(j, int) and j == 0
                    pe.wait_ge(unit_ready, u + 1)
                    bank_free(j)
                    for k in range(KD):
                        if first and ready:
                            ready(k)
                        for t in range(2):
                            b = ts(2 * k + t, P)
                            last = mm3(ps[bank + t][:], w_hi[slot][:, b], w_lo[slot][:, b],
                                       src_hi[:, ts(k, T)], src_lo[:, ts(k, T)], k == 0, k == KD - 1)
                    last.then_inc(unit_done, 1)
                    if first and after_first:
                        after_first()
                return body

            def after_two(sem_, before, per_unit):
                def wait(j):
                    if not (isinstance(j, int) and j < 2):
                        pe.wait_ge(sem_, j * per_unit + (before - per_unit))
                return wait

            def xg_wait(n):
                return lambda k: pe.wait_ge(xg_ready, KD * n + k + 1)

            def ffn(f, n):
                gu_k, down_k = f"gu{f}", f"down{f}"
                later = after_two(pair_free, FREED[gu_k], 1)

                def bank_free(j):
                    if f == 1 and isinstance(j, int) and j < 2:
                        pe.wait_ge(x_new, KD * n - KD + KD - 2 + 2 * j)
                    later(j)
                rolled(pe, KF, pair_unit(BASE[gu_k], PAIR_BASE[gu_k], xg_hi, xg_lo, bank_free, xg_wait(n),
                                         lambda: sum_squares(n)), first=2)

                def down_tile(m, s):
                    bank = BANK_DOWN + s
                    first = isinstance(m, int) and m == 0
                    for half in range(2):
                        u = m * 2 + (BASE[down_k] + half)
                        slot = (BASE[down_k] + half) % 2
                        pe.wait_ge(unit_ready, u + 1)
                        if half == 0 and not (isinstance(m, int) and m < 2):
                            pe.wait_ge(x_new, m + (KD * n - 1))
                        for kk in range(HALF_F):
                            k = half * HALF_F + kk
                            if first:
                                pe.wait_ge(h_ready, KF * f + k + 1)
                            last = mm3(ps[bank][:], w_hi[slot][:, ts(kk, P)], w_lo[slot][:, ts(kk, P)],
                                       h_hi[:, ts(k, T)], h_lo[:, ts(k, T)], k == 0, k == KF - 1)
                        last.then_inc(unit_done, 1)
                rolled(pe, KD, down_tile, first=2)

            def fox(n):
                def first_stats():
                    sum_squares(n)
                    for tt in range(TT):
                        last = pe.matmul(ps[BANK_TOK][:, tt:tt + 1], ssq[:, ts(tt, P)], ones[:, 0:1],
                                         start=True, stop=True)
                    last.then_inc(tok_mm, 1)
                rolled(pe, KD, pair_unit(BASE["qk"], PAIR_BASE["qk"], xg_hi, xg_lo,
                                         after_two(pair_free, FREED["qk"], 1), xg_wait(n), first_stats), first=2)
                u = BASE["f"]
                pe.wait_ge(unit_ready, u + 1)
                for k in range(KD):
                    last = mm3(ps[BANK_F][:], w_hi[u % 2][:, ts(k, P)], w_lo[u % 2][:, ts(k, P)],
                               xg_hi[:, ts(k, T)], xg_lo[:, ts(k, T)], k == 0, k == KD - 1)
                last.then_inc(unit_done, 1)
                for c in range(2):
                    for half in range(2):
                        u = BASE["v"] + 2 * c + half
                        pe.wait_ge(unit_ready, u + 1)
                        if c == 0 and half == 0:
                            pe.wait_ge(f_step, 1)
                            pe.wait_ge(r_ready, n + 1)
                            pe.wait_ge(tok_ready, 1)
                        if c == 1 and half == 0:
                            pe.wait_ge(pair_free, FREED["qk"] + KD)
                        for kk in range(KD // 2):
                            k = half * (KD // 2) + kk
                            for tt in range(TT):
                                at_ = slice(k * T + tt * P, k * T + (tt + 1) * P)
                                wc = ts(kk, T)
                                last = mm3(ps[BANK_V * (1 - c) + tt][:], xg_hi[:, at_], xg_lo[:, at_],
                                           w_hi[u % 2][:, wc], w_lo[u % 2][:, wc], k == 0, k == KD - 1)
                        last.then_inc(unit_done, 1)

                def scores(h, s, i):
                    b, e = (s // 2) % 2, 2 * T * (s % 2)
                    w = (i + 1) * P
                    q_hi, q_lo = (qk_split[b][:, e + a * T + i * P:e + a * T + (i + 1) * P] for a in range(2))
                    k_hi, k_lo = (qk_split[b][:, (4 + a) * T:(4 + a) * T + w] for a in range(2))
                    if i == 0:
                        pe.wait_ge(qk_ready, h + 1)
                        pe.wait_ge(rows_in[s % 2], h * 16 + (32 - 16 * (s % 2)))
                    if isinstance(h, int) and h == 0:
                        pe.wait_ge(v_raw_done, 2 * TT)
                    else:
                        pe.wait_ge(exp_done, h * TT + (i + 1 - TT))
                    mm3(ps[i][:, 0:w], q_hi, q_lo, k_hi, k_lo, True, False)
                    pe.matmul(ps[i][:, 0:w], forget[s % 2][:, ts(i, P)], forget[s % 2][:, T:T + w],
                              start=False, stop=False)
                    pe.matmul(ps[i][:, i * P:w], ident_r[:], mask_r[:], start=False, stop=True)\
                        .then_inc(scores_done, 1)

                def transposes(h, s, i):
                    at_ = P * (i * (i + 1) // 2)
                    pe.wait_ge(prob_ready, h * TT + (i + 1))
                    pe.wait_ge(pt_ready, h * TT + (i + 1))
                    for j in range(i + 1):
                        last = pe.transpose(ps[BANK_PT + i % 2][:, ts(j, P)], prob[:, at_ + j * P:at_ + (j + 1) * P],
                                            ident[:])
                    last.then_inc(pt_done, 1)

                def values(h, s, i):
                    vb, even = (s // 2) % 2, s % 2 == 0
                    if even and i == 1:
                        pe.wait_ge(v_ready, pair_of(h) + 1)
                        pe.wait_ge(o_ready, pair_of(h) + 1)
                    pe.wait_ge(pt_ready, h * TT + (i + 3))
                    for j in range(i + 1):
                        vc = slice((2 * j + s % 2) * P, (2 * j + s % 2 + 1) * P)
                        q0 = max(i - 1, j)
                        n = (i + 1 - q0) * P
                        at_ = (i // 2) * 4 * P + j * 2 * P + (q0 % 2) * P
                        last = mm3(ps[BANK_O + vb][:, q0 * P:(i + 1) * P], v_hi[vb][:, vc], v_lo[vb][:, vc],
                                   pt_hi[:, at_:at_ + n], pt_lo[:, at_:at_ + n], even and i == 1 and j == 0,
                                   not even and i == TT - 1 and j == i)
                    if i == TT - 1 and not even:
                        last.then_inc(pv_done, 1)

                def attend(h, s):
                    for i in range(TT):
                        ahead(transposes, h, s, i + 1)
                        ahead(scores, h, s, i + 5)
                        if i % 2 == 1:
                            values(h, s, i)

                for i in range(TT):
                    scores(0, 0, i)
                scores(1, 1, 0)
                transposes(0, 0, 0)
                rolled(pe, HEADS, attend, first=2, last=2, unroll=4)

                rolled(pe, KD // 2, pair_unit(BASE["fox_out"], PAIR_BASE["fox_out"], o_hi, o_lo,
                                              after_two(x_new, KD * n, 2),
                                              lambda k: pe.wait_ge(o_ready, k + 3)), first=2)

            def lru(n):
                rolled(pe, KR // 2, pair_unit(BASE["rec"], PAIR_BASE["rec"], xg_hi, xg_lo, after_two(rec_ready, 0, 2),
                                              xg_wait(n), lambda: sum_squares(n)), first=2)
                g = 0
                for i in range(4):
                    u = BASE["gates"] + i
                    pe.wait_ge(unit_ready, u + 1)
                    blk = 0
                    for m0 in range(GATE_HALF):
                        m = (i // 2) * GATE_HALF + m0
                        if g >= 4:
                            pe.wait_ge(gate_out, g - 3)
                        elif g == 0:
                            pe.wait_ge(r_ready, n + 1)
                        pe.wait_ge(xc_ready, BAND[m][-1] + 1)
                        for t, k in enumerate(BAND[m]):
                            last = mm3(ps[BANK_GATE + g % 4][:], w_hi[u % 2][:, ts(blk, P)], w_lo[u % 2][:, ts(blk, P)],
                                       xc_hi[:, ts(k, T)], xc_lo[:, ts(k, T)], t == 0, t == len(BAND[m]) - 1)
                            blk += 1
                        last.then_inc(unit_done if m0 == GATE_HALF - 1 else gate_mm, 1)
                        g += 1
                rolled(pe, KR // 2, pair_unit(BASE["gate_br"], PAIR_BASE["gate_br"], xg_hi, xg_lo,
                                              after_two(gt_ready, 0, 2)), first=2)

                def out_tile(m, s):
                    u = m + BASE["lru_out"]
                    slot, bank = (BASE["lru_out"] + s) % 2, BANK_DOWN + s
                    pe.wait_ge(unit_ready, u + 1)
                    if isinstance(m, int) and m < 2:
                        pe.wait_ge(gate_out, 4 * GATE_HALF)
                    else:
                        pe.wait_ge(x_new, m + (KD * n - 1))
                    for k in range(KR):
                        if isinstance(m, int) and m == 0:
                            pe.wait_ge(y_ready, k + 1)
                        last = mm3(ps[bank][:], w_hi[slot][:, ts(k, P)], w_lo[slot][:, ts(k, P)],
                                   xc_hi[:, ts(k, T)], xc_lo[:, ts(k, T)], k == 0, k == KR - 1)
                    last.then_inc(unit_done, 1)
                rolled(pe, KD, out_tile, first=2)

            pe.wait_ge(consts, 7)
            ffn(0, 0)
            fox(1)
            ffn(1, 2)
            ffn(2, 3)
            lru(4)
            ffn(3, 5)
            sum_squares(N_NORMS - 1)

        @block.scalar
        def _(act):
            for k in range(KD // 2, KD):
                act.dma_start(x[:, ts(k, T)], x_t[k]).then_inc(x_tile_in[k], 16)

            def hi_split(u, cols, slot):
                if isinstance(u, int):
                    if u >= N_UNITS:
                        return
                    cols = UNIT_COLS[u]
                act.wait_ge(raw_in[slot], u * 8 + (16 - 8 * slot))
                if not (isinstance(u, int) and u < 2):
                    act.wait_ge(unit_done, u - 1)
                act.activation(w_hi[slot][:, 0:cols], w_raw[slot][:, 0:cols], ACT.Copy).then_inc(hi_done, 1)

            def x_tile(n, m, s):
                c = m + KD * n
                if not (isinstance(c, int) and c < 2):
                    act.wait_ge(ssq_added, c - 1)
                act.wait_ge(x_new, m + (KD * (n - 1) + 1))
                if n < N_NORMS - 1:
                    act.activation(xg_hi[:, ts(m, T)], x[:, ts(m, T)], ACT.Copy, scale=gain(n, m))\
                        .then_inc(xg_hi_done, 1)
                act.activation(sq[:, ts(s, T)], x[:, ts(m, T)], ACT.Square).then_inc(sq_done, 1)

            def root(n):
                act.wait_ge(ssq_mm, n + 1)
                act.activation(r_bc[:], ps[BANK_SSQ][:], ACT.Sqrt, scale=1.0 / D, bias=eps[:]).then_inc(sqrt_done, 1)

            def ffn(f, n):
                gu_k, down_k = f"gu{f}", f"down{f}"

                def gu_unit(j, s):
                    if isinstance(j, int) and j == 0:
                        root(n)
                    hi_split(j + (BASE[gu_k] + 2), PAIR, (BASE[gu_k] + s) % 2)
                    act.wait_ge(g_ready, j + (KF * f + 1))
                    act.activation(g_buf[s][:], g_buf[s][:], ACT.Silu).then_inc(silu_done, 1)
                rolled(act, KF, gu_unit, first=2, last=2)

                def down_tile(m, s):
                    u = m * 2 + (BASE[down_k] + 2)
                    hi_split(u, DOWN, BASE[down_k] % 2)
                    x_tile(n + 1, m, s)
                    hi_split(u + 1, DOWN, (BASE[down_k] + 1) % 2)
                rolled(act, KD, down_tile, last=2)

            def fox(n):
                def qk_unit(j, s):
                    if isinstance(j, int) and j == 0:
                        root(n)
                        act.wait_ge(tok_mm, 1)
                        act.activation(r_tok[:], ps[BANK_TOK][:, 0:TT], ACT.Sqrt, scale=1.0 / D, bias=eps[:])\
                            .then_inc(tok_sqrt, 1)
                    hi_split(j + (BASE["qk"] + 2), PAIR, (BASE["qk"] + s) % 2)
                rolled(act, KD, qk_unit, first=2, last=2)
                hi_split(BASE["f"] + 2, 0, BASE["f"] % 2)
                act.wait_ge(f_step, 2)
                act.activation(fl_b[:], fl_a[:], ACT.Abs).then_inc(f_exp, 1)
                act.wait_ge(f_exp, 1)
                act.activation(fl_b[:], fl_b[:], ACT.Exp, scale=-1.0).then_inc(f_exp, 1)
                act.wait_ge(f_exp, 2)
                act.activation(fl_b[:], fl_b[:], ACT.Ln, scale=1.0, bias=ones[0:HEADS, 0:1]).then_inc(f_exp, 1)
                for i in range(4):
                    u = BASE["v"] + i
                    hi_split(u + 2, 0, u % 2)
                    if i % 2 == 1:
                        c = i // 2
                        act.wait_ge(unit_done, u + 1)
                        act.wait_ge(tok_ready, 1)
                        for tt in range(TT):
                            act.activation(v_raw[:, tt * D + c * T:tt * D + (c + 1) * T], ps[BANK_V * (1 - c) + tt][:],
                                           ACT.Copy, scale=r_tok[:, tt:tt + 1]).then_inc(v_raw_done, 1)

                def q_split(pair, b, e):
                    ro = slice(HEAD_DIM * e, HEAD_DIM * (e + 1))
                    act.activation(qk_split[b][ro, 2 * e * T:(2 * e + 1) * T], q_raw[ro, ts(pair, T)], ACT.Copy,
                                   scale=HEAD_DIM ** -0.5).then_inc(qk_hi_done, 1)

                def k_split(pair, b):
                    act.activation(qk_split[b][:, 4 * T:5 * T], k_raw[:, ts(pair, T)], ACT.Copy).then_inc(qk_hi_done, 1)

                def v_split(pair, b):
                    act.activation(v_view(v_hi[b][:]), v_of_pair(pair), ACT.Copy).then_inc(v_hi_done, 1)

                def exp_block(h, s, i):
                    w, at_ = (i + 1) * P, P * (i * (i + 1) // 2)
                    act.wait_ge(max_done, h * TT + (i + 1))
                    act.activation(prob[:, at_:at_ + w], ps[i][:, 0:w], ACT.Exp, bias=neg_max[:, i:i + 1],
                                   accum_out=row_sum[:, i:i + 1]).then_inc(exp_done, 1)

                def pt_high(h, s, i):
                    w = (i + 1) * P
                    act.wait_ge(pt_done, h * TT + (i + 1))
                    src = ps[BANK_PT + i % 2][:, 0:w].rearrange("p (j n) -> p j n", n=P)
                    act.activation(pt_block(pt_hi, i), src, ACT.Copy).then_inc(pt_hi_done, 1)

                def o_split(pair, b):
                    act.activation(o_hi[:, ts(pair, T)], ps[BANK_O + b][:], ACT.Copy).then_inc(o_hi_done, 1)

                def attend(h, s):
                    nb = (s // 2 + 1) % 2
                    more = not (isinstance(h, int) and h + 2 >= HEADS)
                    for i in range(TT):
                        ahead(exp_block, h, s, i + 3)
                        ahead(pt_high, h, s, i + 1)
                        if more and (s % 2, i) == (0, 0):
                            q_split(pair_of(h) + 1, nb, 0)
                        if more and (s % 2, i) == (0, 2):
                            k_split(pair_of(h) + 1, nb)
                        if (s % 2, i) == (0, 3) and not (isinstance(h, int) and h == 0):
                            o_split(pair_of(h) - 1, nb)
                        if more and (s % 2, i) == (1, 0):
                            q_split(pair_of(h) + 1, nb, 1)
                        if more and (s % 2, i) == (1, 2):
                            v_split(pair_of(h) + 1, nb)

                act.wait_ge(pair_free, FREED["qk"] + KD)
                act.wait_ge(pads, 10)
                q_split(0, 0, 0)
                k_split(0, 0)
                q_split(0, 0, 1)
                act.wait_ge(v_raw_done, 2 * TT)
                v_split(0, 0)
                exp_block(0, 0, 0)
                exp_block(0, 0, 1)
                pt_high(0, 0, 0)
                exp_block(0, 0, 2)
                act.wait_ge(pads, 14)
                rolled(act, HEADS, attend, first=2, last=2, unroll=4)
                act.wait_ge(pv_done, HEADS // 2)
                o_split(HEADS // 2 - 1, (HEADS // 2 - 1) % 2)

                def out_unit(j, s):
                    hi_split(j + (BASE["fox_out"] + 2), PAIR, (BASE["fox_out"] + s) % 2)
                    for t in range(2):
                        x_tile(n + 1, j * 2 + t, t)
                rolled(act, KD // 2, out_unit, last=2)

            def lru(n):
                def rec_unit(j, s):
                    if isinstance(j, int) and j == 0:
                        root(n)
                    hi_split(j + (BASE["rec"] + 2), PAIR, (BASE["rec"] + s) % 2)
                    for t in range(2):
                        m = j * 2 + t
                        act.wait_ge(rec_ready, m + 1)
                        act.activation(xc[:, ts(m, T)], rec_pad[t][:, 0:T], ACT.Identity,
                                       scale=par[:, bass.ds(m + COL_CONV_W, 1)],
                                       bias=par[:, bass.ds(m + COL_CONV_B, 1)]).then_inc(tap0_done, 1)
                    for t in range(2):
                        m = j * 2 + t
                        act.wait_ge(conv_step, j * 6 + (5 + t))
                        act.activation(xc_hi[:, ts(m, T)], xc[:, ts(m, T)], ACT.Copy).then_inc(xc_hi_done, 1)
                for j in range(KR // 2):
                    rec_unit(j, j % 2)
                g = 0
                for i in range(4):
                    for m0 in range(GATE_HALF):
                        m = (i // 2) * GATE_HALF + m0
                        if m0 == GATE_HALF - 1:
                            act.wait_ge(unit_done, BASE["gates"] + i + 1)
                        else:
                            act.wait_ge(gate_mm, i * (GATE_HALF - 1) + m0 + 1)
                        if i % 2 == 0:
                            act.activation(r_gate[:, ts(m, T)], ps[BANK_GATE + g % 4][:], ACT.Sigmoid,
                                           bias=col(COL_B_A, m)).then_inc(gate_out, 1)
                        else:
                            if m >= 2:
                                act.wait_ge(gi_used, m - 1)
                            act.activation(gi[m % 2][:], ps[BANK_GATE + g % 4][:], ACT.Sigmoid,
                                           bias=col(COL_B_I, m)).then_inc(gate_out, 1)
                        g += 1
                    hi_split(BASE["gates"] + i + 2, 0, (BASE["gates"] + i) % 2)
                act.wait_ge(gate_out, 4 * GATE_HALF)
                for m in range(KR):
                    act.activation(q_lru[:, ts(m, T)], r_gate[:, ts(m, T)], ACT.Tanh, scale=lru_nc[:, m:m + 1])\
                        .then_inc(tanh_done, 1)
                    act.activation(r_gate[:, ts(m, T)], r_gate[:, ts(m, T)], ACT.Exp, scale=lru_c[:, m:m + 1])\
                        .then_inc(a_done, 1)

                def gelu(m):
                    act.wait_ge(gt_ready, m + 1)
                    act.activation(gt[:, ts(m, T)], gt[:, ts(m, T)], ACT.Gelu_apprx_tanh).then_inc(gelu_done, 1)

                def y_high(m):
                    act.wait_ge(y_made, m + 1)
                    act.activation(xc_hi[:, ts(m, T)], xc[:, ts(m, T)], ACT.Copy).then_inc(y_hi_done, 1)

                for j in range(KR // 2):
                    hi_split(BASE["gate_br"] + j + 2, 0, (BASE["gate_br"] + j) % 2)
                    if j == 1:
                        for m in range(KR):
                            act.wait_ge(q_done, m + 1)
                            act.activation(q_lru[:, ts(m, T)], q_lru[:, ts(m, T)], ACT.Sqrt).then_inc(root_done, 1)
                    if j >= 2:
                        new = range(0, 6) if j == 2 else range(2 * j, 2 * j + 2)
                        for m in new:
                            gelu(m)
                        for m in new:
                            y_high(m)

                def out_tile(m, s):
                    hi_split(m + (BASE["lru_out"] + 2), COLS["lru_out"], (BASE["lru_out"] + s) % 2)
                    x_tile(n + 1, m, s)
                rolled(act, KD, out_tile, last=2)

            act.wait_ge(par_in, 16)
            act.activation(sp[:, 0:KR], par[:, COL_LAMBDA:COL_LAMBDA + KR], ACT.Abs).then_inc(lam_exp, 1)
            act.wait_ge(lam_exp, 1)
            act.activation(sp[:, KR:2 * KR], sp[:, 0:KR], ACT.Exp, scale=-1.0).then_inc(lam_exp, 1)
            hi_split(0, 0, 0)
            for m in range(KD):
                act.wait_ge(x_tile_in[m], 16)
                act.activation(xg_hi[:, ts(m, T)], x[:, ts(m, T)], ACT.Copy, scale=gain(0, m)).then_inc(xg_hi_done, 1)
                if m >= 2:
                    act.wait_ge(ssq_added, m - 1)
                act.activation(sq[:, ts(m % 2, T)], x[:, ts(m, T)], ACT.Square).then_inc(sq_done, 1)
                if m == 1:
                    hi_split(1, 0, 1)
            act.wait_ge(consts, 7)
            ffn(0, 0)
            fox(1)
            ffn(1, 2)
            ffn(2, 3)
            lru(4)
            ffn(3, 5)
            root(N_NORMS - 1)

        @block.vector
        def _(dve):
            def lo_split(u, cols, slot):
                if isinstance(u, int):
                    if u >= N_UNITS:
                        return
                    cols = UNIT_COLS[u]
                dve.wait_ge(hi_done, u + 1)
                dve.tensor_tensor(w_lo[slot][:, 0:cols], w_raw[slot][:, 0:cols], f32(w_hi[slot][:, 0:cols]),
                                  ALU.subtract).then_inc(unit_ready, 1)

            def norm_low(n, m):
                c = m + KD * n
                if n < N_NORMS - 1:
                    dve.wait_ge(xg_hi_done, c + 1)
                    dve.scalar_tensor_tensor(out=xg_lo[:, ts(m, T)], in0=x[:, ts(m, T)], scalar=gain(n, m),
                                             in1=f32(xg_hi[:, ts(m, T)]), op0=ALU.mult, op1=ALU.subtract)\
                        .then_inc(xg_ready, 1)

            def add_square(n, m, s):
                c = m + KD * n
                dve.wait_ge(sq_done, c + 1)
                dve.wait_ge(ssq_added, c) if not (isinstance(c, int) and c == 0) else None
                dve.tensor_tensor(ssq[:], ssq[:], sq[:, ts(s, T)], ALU.add).then_inc(ssq_added, 1)

            def update_x(n, m, bank, factor):
                dve.scalar_tensor_tensor(out=x[:, ts(m, T)], in0=ps[bank][:], scalar=factor, in1=x[:, ts(m, T)],
                                         op0=ALU.mult, op1=ALU.add).then_inc(x_new, 1)

            def make_r(n):
                dve.wait_ge(sqrt_done, n + 1)
                dve.reciprocal(r_bc[:], r_bc[:]).then_inc(r_ready, 1)
                if n == 1:
                    dve.wait_ge(tok_mm, 1)
                dve.memset(ssq[:], 0.0).then_inc(ssq_zero, 1)
                dve.wait_ge(r_ready, n + 1)
                dve.wait_ge(ssq_zero, n + 2)

            def ffn(f, n):
                gu_k, down_k = f"gu{f}", f"down{f}"

                def gu_unit(j, s):
                    c = j + KF * f
                    bank = 2 * ((PAIR_BASE[gu_k] + s) % 2)
                    if isinstance(j, int) and j == 0:
                        make_r(n)
                    dve.wait_ge(unit_done, j + (BASE[gu_k] + 1))
                    dve.tensor_tensor(g_buf[s][:], ps[bank][:], r_bc[:], ALU.mult).then_inc(g_ready, 1)
                    dve.tensor_tensor(u_buf[s][:], ps[bank + 1][:], r_bc[:], ALU.mult).then_inc(pair_free, 1)
                    lo_split(j + (BASE[gu_k] + 2), PAIR, (BASE[gu_k] + s) % 2)
                    dve.wait_ge(silu_done, c + 1)
                    dve.wait_ge(pair_free, j + (FREED[gu_k] + 1))
                    dve.tensor_tensor(u_buf[s][:], g_buf[s][:], u_buf[s][:], ALU.mult).then_inc(h_made, 1)
                    dve.wait_ge(h_made, c + 1)
                    dve.tensor_copy(h_hi[:, ts(j, T)], u_buf[s][:]).then_inc(h_hi_done, 1)
                    dve.wait_ge(h_hi_done, c + 1)
                    dve.tensor_tensor(h_lo[:, ts(j, T)], u_buf[s][:], f32(h_hi[:, ts(j, T)]), ALU.subtract)\
                        .then_inc(h_ready, 1)
                rolled(dve, KF, gu_unit, first=2, last=2)

                def down_tile(m, s):
                    u = m * 2 + (BASE[down_k] + 2)
                    lo_split(u, DOWN, BASE[down_k] % 2)
                    dve.wait_ge(unit_done, u)
                    update_x(n + 1, m, BANK_DOWN + s, 0.5)
                    norm_low(n + 1, m)
                    add_square(n + 1, m, s)
                    lo_split(u + 1, DOWN, (BASE[down_k] + 1) % 2)
                rolled(dve, KD, down_tile, last=2)

            def fox(n):
                def qk_unit(j, s):
                    bank = 2 * ((PAIR_BASE["qk"] + s) % 2)
                    if isinstance(j, int) and j == 0:
                        make_r(n)
                        dve.wait_ge(tok_sqrt, 1)
                        dve.reciprocal(r_tok[:], r_tok[:]).then_inc(tok_ready, 1)
                    dve.wait_ge(unit_done, j + (BASE["qk"] + 1))
                    dve.tensor_tensor(q_raw[:, ts(j, T)], ps[bank][:], r_bc[:], ALU.mult)
                    dve.tensor_tensor(k_raw[:, ts(j, T)], ps[bank + 1][:], r_bc[:], ALU.mult).then_inc(pair_free, 1)
                    lo_split(j + (BASE["qk"] + 2), PAIR, (BASE["qk"] + s) % 2)
                rolled(dve, KD, qk_unit, first=2, last=2)

                dve.wait_ge(unit_done, BASE["f"] + 1)
                hp = slice(0, HEADS)
                dve.tensor_tensor(fl_a[:], ps[BANK_F][hp, :], r_bc[hp, :], ALU.mult).then_inc(f_step, 1)
                dve.wait_ge(f_step, 1)
                dve.tensor_scalar(fl_a[:], fl_a[:], par[hp, COL_B_F:COL_B_F + 1], None, ALU.add).then_inc(f_step, 1)
                lo_split(BASE["f"] + 2, 0, BASE["f"] % 2)
                dve.memset(fl_c[:], 1.0).then_inc(f_step, 1)
                dve.wait_ge(f_exp, 3)
                dve.scalar_tensor_tensor(out=fl_a[:], in0=fl_a[:], scalar=0.0, in1=fl_b[:], op0=ALU.min,
                                         op1=ALU.subtract).then_inc(f_step, 1)
                dve.wait_ge(f_step, 4)
                dve.tensor_tensor_scan(fl_b[:], fl_c[:], fl_a[:], 0.0, ALU.mult, ALU.add).then_inc(f_step, 1)
                dve.wait_ge(f_step, 5)
                high, low = slice(0, HEADS), slice(32, 32 + HEADS)
                dve.tensor_copy(f_pack[high, 0:T], fl_b[:]).then_inc(f_step, 1)
                dve.wait_ge(f_step, 6)
                dve.tensor_tensor(f_pack[low, 0:T], fl_b[:], f32(f_pack[high, 0:T]), ALU.subtract).then_inc(f_step, 1)
                dve.wait_ge(f_step, 7)
                for part in (high, low):
                    dve.tensor_scalar(f_pack[part, T:2 * T], f32(f_pack[part, 0:T]), -1.0, None, ALU.mult)\
                        .then_inc(f_packed, 1)
                for i in range(4):
                    lo_split(BASE["v"] + i + 2, 0, (BASE["v"] + i) % 2)

                def q_split(pair, b, e, n_hi):
                    ro = slice(HEAD_DIM * e, HEAD_DIM * (e + 1))
                    dve.wait_ge(qk_hi_done, pair * 3 + n_hi)
                    low = dve.scalar_tensor_tensor(out=qk_split[b][ro, (2 * e + 1) * T:(2 * e + 2) * T],
                                                  in0=q_raw[ro, ts(pair, T)], scalar=HEAD_DIM ** -0.5,
                                                  in1=f32(qk_split[b][ro, 2 * e * T:(2 * e + 1) * T]),
                                                  op0=ALU.mult, op1=ALU.subtract)
                    if e == 1:
                        low.then_inc(qk_ready, 1)

                def k_split(pair, b):
                    dve.wait_ge(qk_hi_done, pair * 3 + 2)
                    dve.tensor_tensor(qk_split[b][:, 5 * T:6 * T], k_raw[:, ts(pair, T)],
                                      f32(qk_split[b][:, 4 * T:5 * T]), ALU.subtract).then_inc(qk_ready, 1)

                def v_split(pair, b):
                    dve.wait_ge(v_hi_done, pair + 1)
                    dve.tensor_tensor(v_view(v_lo[b][:]), v_of_pair(pair), v_view(f32(v_hi[b][:])), ALU.subtract)\
                        .then_inc(v_ready, 1)

                def max_block(h, s, i):
                    dve.wait_ge(scores_done, h * TT + (i + 1))
                    dve.tensor_reduce(neg_max[:, i:i + 1], ps[i][:, 0:(i + 1) * P], AX.X, ALU.max,
                                      negate=True).then_inc(max_done, 1)

                def normalise(h, s, i):
                    w, at_ = (i + 1) * P, P * (i * (i + 1) // 2)
                    dve.wait_ge(exp_done, h * TT + (i + 1))
                    dve.reciprocal(row_rcp[:, i:i + 1], row_sum[:, i:i + 1]).then_inc(rcp_done, 1)
                    dve.wait_ge(rcp_done, h * TT + (i + 1))
                    dve.tensor_scalar(prob[:, at_:at_ + w], prob[:, at_:at_ + w], row_rcp[:, i:i + 1], None, ALU.mult)\
                        .then_inc(prob_ready, 1)

                def pt_low(h, s, i):
                    w = (i + 1) * P
                    src = ps[BANK_PT + i % 2][:, 0:w].rearrange("p (j n) -> p j n", n=P)
                    dve.wait_ge(pt_hi_done, h * TT + (i + 1))
                    dve.tensor_tensor(pt_block(pt_lo, i), src, f32(pt_block(pt_hi, i)), ALU.subtract).then_inc(pt_ready, 1)

                def o_split(pair, b):
                    dve.wait_ge(o_hi_done, pair + 1)
                    dve.tensor_tensor(o_lo[:, ts(pair, T)], ps[BANK_O + b][:], f32(o_hi[:, ts(pair, T)]),
                                      ALU.subtract).then_inc(o_ready, 1)

                def attend(h, s):
                    nb = (s // 2 + 1) % 2
                    more = not (isinstance(h, int) and h + 2 >= HEADS)
                    for i in range(TT):
                        ahead(normalise, h, s, i + 2)
                        ahead(max_block, h, s, i + 4)
                        ahead(pt_low, h, s, i + 1)
                        if more and (s % 2, i) == (0, 0):
                            q_split(pair_of(h) + 1, nb, 0, 1)
                        if more and (s % 2, i) == (0, 2):
                            k_split(pair_of(h) + 1, nb)
                        if (s % 2, i) == (0, 3) and not (isinstance(h, int) and h == 0):
                            o_split(pair_of(h) - 1, nb)
                        if more and (s % 2, i) == (1, 0):
                            q_split(pair_of(h) + 1, nb, 1, 3)
                        if more and (s % 2, i) == (1, 2):
                            v_split(pair_of(h) + 1, nb)

                q_split(0, 0, 0, 1)
                k_split(0, 0)
                q_split(0, 0, 1, 3)
                v_split(0, 0)
                max_block(0, 0, 0)
                max_block(0, 0, 1)
                normalise(0, 0, 0)
                max_block(0, 0, 2)
                normalise(0, 0, 1)
                max_block(0, 0, 3)
                pt_low(0, 0, 0)
                rolled(dve, HEADS, attend, first=2, last=2, unroll=4)
                o_split(HEADS // 2 - 1, (HEADS // 2 - 1) % 2)

                def out_unit(j, s):
                    bank = 2 * ((PAIR_BASE["fox_out"] + s) % 2)
                    dve.wait_ge(unit_done, j + (BASE["fox_out"] + 1))
                    for t in range(2):
                        update_x(n + 1, j * 2 + t, bank + t, 1.0)
                    norm_low(n + 1, j * 2)
                    dve.wait_ge(xg_hi_done, j * 2 + (KD * (n + 1) + 2))
                    m = j * 2 + 1
                    dve.scalar_tensor_tensor(out=xg_lo[:, ts(m, T)], in0=x[:, ts(m, T)], scalar=gain(n + 1, m),
                                             in1=f32(xg_hi[:, ts(m, T)]), op0=ALU.mult, op1=ALU.subtract)\
                        .then_inc(xg_ready, 1)
                    add_square(n + 1, j * 2, 0)
                    add_square(n + 1, m, 1)
                    lo_split(j + (BASE["fox_out"] + 2), PAIR, (BASE["fox_out"] + s) % 2)
                rolled(dve, KD // 2, out_unit, last=2)

            def lru(n):
                dve.memset(rec_pad[0][:, 0:TAPS - 1], 0.0)
                dve.memset(rec_pad[1][:, 0:TAPS - 1], 0.0)

                def rec_unit(j, s):
                    bank = 2 * ((PAIR_BASE["rec"] + s) % 2)
                    if isinstance(j, int) and j == 0:
                        make_r(n)
                    dve.wait_ge(unit_done, j + (BASE["rec"] + 1))
                    for t in range(2):
                        dve.tensor_tensor(rec_pad[t][:, TAPS - 1:TAPS - 1 + T], ps[bank + t][:], r_bc[:], ALU.mult)\
                            .then_inc(rec_ready, 1)
                    lo_split(j + (BASE["rec"] + 2), PAIR, (BASE["rec"] + s) % 2)
                    for tap in range(1, TAPS):
                        for t in range(2):
                            m = j * 2 + t
                            if tap == 1:
                                dve.wait_ge(tap0_done, m + 1)
                            else:
                                dve.wait_ge(conv_step, conv_count(j, tap - 1, t))
                            xm = xc[:, ts(m, T)]
                            dve.scalar_tensor_tensor(out=xm, in0=rec_pad[t][:, tap:tap + T],
                                                     scalar=par[:, bass.ds(m + (COL_CONV_W + tap * KR), 1)],
                                                     in1=xm, op0=ALU.mult, op1=ALU.add).then_inc(conv_step, 1)
                    for t in range(2):
                        m = j * 2 + t
                        dve.wait_ge(xc_hi_done, m + 1)
                        dve.tensor_tensor(xc_lo[:, ts(m, T)], xc[:, ts(m, T)], f32(xc_hi[:, ts(m, T)]), ALU.subtract)\
                            .then_inc(xc_ready, 1)

                def conv_count(j, tap, t):
                    return j * 6 + (2 * (tap - 1) + t + 1)

                for j in range(KR // 2):
                    rec_unit(j, j % 2)
                g = 0
                for i in range(4):
                    for m0 in range(GATE_HALF):
                        m = (i // 2) * GATE_HALF + m0
                        g += 1
                        if i % 2 == 1:
                            dve.wait_ge(gate_out, g)
                            dve.tensor_tensor(xc[:, ts(m, T)], gi[m % 2][:], xc[:, ts(m, T)], ALU.mult).then_inc(gi_used, 1)
                    lo_split(BASE["gates"] + i + 2, 0, (BASE["gates"] + i) % 2)

                def one_minus_a2(m):
                    qm = q_lru[:, ts(m, T)]
                    dve.wait_ge(tanh_done, m + 1)
                    if m:
                        dve.wait_ge(q_done, m)
                    dve.tensor_scalar(den[:], qm, 1.0, None, ALU.add).then_inc(q_step, 1)
                    dve.wait_ge(q_step, 2 * m + 1)
                    dve.reciprocal(den[:], den[:]).then_inc(q_step, 1)
                    dve.wait_ge(q_step, 2 * m + 2)
                    dve.scalar_tensor_tensor(out=qm, in0=qm, scalar=2.0, in1=den[:], op0=ALU.mult, op1=ALU.mult)\
                        .then_inc(q_done, 1)

                def recur(m):
                    xm, qm = xc[:, ts(m, T)], q_lru[:, ts(m, T)]
                    dve.wait_ge(root_done, m + 1)
                    dve.tensor_tensor(xm, qm, xm, ALU.mult).then_inc(b_done, 1)
                    dve.wait_ge(b_done, m + 1)
                    dve.wait_ge(a_done, m + 1)
                    dve.tensor_tensor_scan(qm, r_gate[:, ts(m, T)], xm, 0.0, ALU.mult, ALU.add).then_inc(scan_done, 1)

                def gated(m):
                    dve.wait_ge(scan_done, m + 1)
                    dve.wait_ge(gelu_done, m + 1)
                    dve.tensor_tensor(xc[:, ts(m, T)], q_lru[:, ts(m, T)], gt[:, ts(m, T)], ALU.mult).then_inc(y_made, 1)

                def y_low(m):
                    dve.wait_ge(y_hi_done, m + 1)
                    dve.tensor_tensor(xc_lo[:, ts(m, T)], xc[:, ts(m, T)], f32(xc_hi[:, ts(m, T)]), ALU.subtract)\
                        .then_inc(y_ready, 1)

                for m in range(0, 4):
                    one_minus_a2(m)
                for j in range(KR // 2):
                    bank = 2 * ((PAIR_BASE["gate_br"] + j) % 2)
                    dve.wait_ge(unit_done, BASE["gate_br"] + j + 1)
                    for t in range(2):
                        dve.tensor_tensor(gt[:, ts(2 * j + t, T)], ps[bank + t][:], r_bc[:], ALU.mult).then_inc(gt_ready, 1)
                    lo_split(BASE["gate_br"] + j + 2, 0, (BASE["gate_br"] + j) % 2)
                    if j < 2:
                        for m in range(4 + 3 * j, 7 + 3 * j):
                            one_minus_a2(m)
                    if j == 2:
                        for m in range(0, 6):
                            recur(m)
                    if j == 3:
                        for m in range(6, KR):
                            recur(m)
                    if j >= 2:
                        new = range(0, 6) if j == 2 else range(2 * j, 2 * j + 2)
                        for m in new:
                            gated(m)
                        for m in new:
                            y_low(m)

                def out_tile(m, s):
                    dve.wait_ge(unit_done, m + (BASE["lru_out"] + 1))
                    update_x(n + 1, m, BANK_DOWN + s, 1.0)
                    norm_low(n + 1, m)
                    add_square(n + 1, m, s)
                    lo_split(m + (BASE["lru_out"] + 2), COLS["lru_out"], (BASE["lru_out"] + s) % 2)
                rolled(dve, KD, out_tile, last=2)

            dve.memset(ssq[:], 0.0).then_inc(ssq_zero, 1)
            dve.wait_ge(par_in, 16)
            lam = par[:, COL_LAMBDA:COL_LAMBDA + KR]
            dve.wait_ge(ssq_zero, 1)
            lo_split(0, 0, 0)
            for m in range(KD):
                norm_low(0, m)
                add_square(0, m, m % 2)
                if m == 1:
                    lo_split(1, 0, 1)

            e, s_, s2, pl = (sp[:, ts(i, KR)] for i in (1, 2, 3, 4))
            n_step = [0]

            def step(ins):
                n_step[0] += 1
                ins.then_inc(lam_step, 1)
                dve.wait_ge(lam_step, n_step[0])
            dve.wait_ge(lam_exp, 2)
            step(dve.tensor_scalar(s_, e, 2.0, None, ALU.add))
            step(dve.reciprocal(s_, s_))
            step(dve.tensor_tensor(s_, e, s_, ALU.mult))
            step(dve.tensor_tensor(s2, s_, s_, ALU.mult))
            step(dve.tensor_scalar(pl, s2, 1.0 / 17, None, ALU.mult))
            for k in (15, 13, 11, 9, 7, 5, 3):
                step(dve.scalar_tensor_tensor(out=pl, in0=pl, scalar=1.0 / k, in1=s2, op0=ALU.add, op1=ALU.mult))
            step(dve.scalar_tensor_tensor(out=pl, in0=pl, scalar=1.0, in1=s_, op0=ALU.add, op1=ALU.mult))
            step(dve.tensor_scalar(s2, lam, -1.0, 0.0, ALU.mult, ALU.max))
            step(dve.scalar_tensor_tensor(out=pl, in0=pl, scalar=2.0, in1=s2, op0=ALU.mult, op1=ALU.add))
            step(dve.tensor_scalar(lru_c[:], pl, -RG_C, None, ALU.mult))
            step(dve.tensor_scalar(lru_nc[:], pl, RG_C, None, ALU.mult))
            ffn(0, 0)
            fox(1)
            ffn(1, 2)
            ffn(2, 3)
            lru(4)
            ffn(3, 5)
            make_r(N_NORMS - 1)
            for m in range(KD):
                dve.scalar_tensor_tensor(out=x[:, ts(m, T)], in0=x[:, ts(m, T)], scalar=gain(N_NORMS - 1, m),
                                         in1=r_bc[:], op0=ALU.mult, op1=ALU.mult).then_inc(out_made, 1)


def lay_out(a):
    def pairs(w, groups, n):
        if groups == 2:
            return w.reshape(KD, P, 2, n, P).transpose(3, 1, 0, 2, 4).reshape(n, P, PAIR)
        return w.reshape(KD, P, n, 2, P).transpose(2, 1, 0, 3, 4).reshape(n, P, PAIR)

    def interleave(w1, w2):
        return [w[i] for i in range(DEPTH) for w in (w1, w2)]

    cols = []
    norms = [g for i in range(DEPTH) for g in (a["ffn1_norm"][i], a["mix_norm"][i], a["ffn2_norm"][i])]
    for g in norms + [a["final_norm"]]:
        cols.append(g.reshape(KD, P).T)
    cols += [a["lru_conv_w"][0, j].reshape(KR, P).T for j in range(TAPS)]
    cols += [a[k][0].reshape(KR, P).T for k in ("lru_conv_b", "lru_b_a", "lru_b_i", "lru_lambda")]
    b_f = np.zeros((P, 1), np.float32)
    b_f[:HEADS, 0] = a["fox_b_f"][0]
    params = np.concatenate(cols + [b_f], 1)

    w_in = a["fox_w_in"][0]
    f_w = np.zeros((KD, P, P), np.float32)
    f_w[:, :, :HEADS] = w_in[:, 3 * D:].reshape(KD, P, HEADS)
    gates = []
    dense = []
    for w in (a["lru_w_a"][0], a["lru_w_i"][0]):
        full = np.zeros((R, R), np.float32)
        for b in range(LRU_BLOCKS):
            at = slice(b * LRU_BLOCK, (b + 1) * LRU_BLOCK)
            full[at, at] = w[b]
        dense.append(full)
    for half in range(2):
        for full in dense:
            gates.append(np.concatenate([full[k * P:(k + 1) * P, m * P:(m + 1) * P]
                                         for m in range(half * GATE_HALF, (half + 1) * GATE_HALF) for k in BAND[m]], 1))
    lru_in = a["lru_w_in"][0]
    return {
        "x_t": a["x"][0].T.reshape(KD, P, T),
        "params": params,
        "gu": np.stack([pairs(w, 2, KF) for w in interleave(a["ffn1_w_gu"], a["ffn2_w_gu"])]),
        "down": np.stack([w.reshape(2, HALF_F, P, KD, P).transpose(3, 0, 2, 1, 4).reshape(2 * KD, P, DOWN)
                          for w in interleave(a["ffn1_w_down"], a["ffn2_w_down"])]),
        "qk": pairs(w_in[:, :2 * D], 2, KD),
        "f_w": f_w.transpose(1, 0, 2).reshape(1, P, KD * P),
        "v_w": w_in[:, 2 * D:3 * D].reshape(2, KD // 2, P, 2, T).transpose(3, 0, 2, 1, 4).reshape(4, P, PAIR),
        "fox_out": pairs(a["fox_w_out"][0], 1, KD // 2),
        "rec": pairs(lru_in[:, R:], 1, KR // 2),
        "gates": np.stack(gates),
        "gate_br": pairs(lru_in[:, :R], 1, KR // 2),
        "lru_out": a["lru_w_out"][0].reshape(KR, P, KD, P).transpose(2, 1, 0, 3).reshape(KD, P, KR * P),
    }


def kernel(**inputs):
    import concourse.bacc as _bacc
    from concourse.bass_utils import run_bass_kernel_spmd as _run

    nc = _bacc.Bacc("TRN2", target_bir_lowering=False, num_devices=1)
    arrays, args = {}, []
    for name, a in lay_out({k: np.asarray(v) for k, v in inputs.items()}).items():
        a = np.ascontiguousarray(a)
        arrays[f"in_{name}_dram"] = a
        args.append(nc.dram_tensor(f"in_{name}_dram", a.shape, mybir.dt.from_np(a.dtype), kind="ExternalInput").ap())
    args.append(nc.dram_tensor("out_dram", (KD, P, T), F32, kind="ExternalOutput").ap())
    build_trunk(nc, *args)
    r = _run(nc, [arrays], core_ids=[0])
    return np.ascontiguousarray(r.results[0]["out_dram"].reshape(D, T).T)[None]
```

```python
from contextlib import ExitStack

import numpy as np

import concourse.bass as bass
from concourse import mybir

F32 = mybir.dt.float32
F32R = mybir.dt.float32r
ALU = mybir.AluOpType
ACT = mybir.ActivationFunctionType
AX = mybir.AxisListType
ts = bass.ts

P = 128
T = 512
D = 1024
DEPTH = 2
HEADS = 16
HEAD_DIM = D // HEADS
R = (4 * D // 3) // 128 * 128
LRU_BLOCKS = 16
LRU_BLOCK = R // LRU_BLOCKS
TAPS = 4
RG_C = 8.0
D_FF = (8 * D // 3 + 255) // 256 * 256
EPS = 1e-6

KD = D // P
KF = D_FF // P
KR = R // P
TT = T // P
HALF_F = KF // 2
N_FFN = 2 * DEPTH
N_NORMS = 3 * DEPTH + 1
MASKED = -1e30

GATE_HALF = 5
BAND = [[i for i in range(KR)
         if any(b * LRU_BLOCK < (m + 1) * P and (b + 1) * LRU_BLOCK > m * P
                and b * LRU_BLOCK < (i + 1) * P and (b + 1) * LRU_BLOCK > i * P
                for b in range(LRU_BLOCKS))] for m in range(KR)]
GATE_BLOCKS = sum(len(BAND[m]) for m in range(GATE_HALF))

COL_GAIN = 0
COL_CONV_W = COL_GAIN + N_NORMS * KD
COL_CONV_B = COL_CONV_W + TAPS * KR
COL_B_A = COL_CONV_B + KR
COL_B_I = COL_B_A + KR
COL_LAMBDA = COL_B_I + KR
COL_B_F = COL_LAMBDA + KR
N_PARAMS = COL_B_F + 1

PAIR = 2 * KD * P
DOWN = HALF_F * P
STREAM = [
    ("gu0", KF, PAIR), ("down0", 2 * KD, DOWN),
    ("qk", KD, PAIR), ("f", 1, KD * P), ("v", 4, PAIR), ("fox_out", KD // 2, PAIR),
    ("gu1", KF, PAIR), ("down1", 2 * KD, DOWN),
    ("gu2", KF, PAIR), ("down2", 2 * KD, DOWN),
    ("rec", KR // 2, PAIR), ("gates_low", 2, GATE_BLOCKS * P), ("gate_br_first", 1, PAIR),
    ("gates_high", 2, GATE_BLOCKS * P), ("gate_br_rest", KR // 2 - 1, PAIR),
    ("lru_out", KD, KR * P),
    ("gu3", KF, PAIR), ("down3", 2 * KD, DOWN),
]
BASE, COLS, UNIT_COLS = {}, {}, []
for _kind, _n, _cols in STREAM:
    BASE[_kind], COLS[_kind] = len(UNIT_COLS), _cols
    UNIT_COLS += [_cols] * _n
N_UNITS = len(UNIT_COLS)

PAIR_BASE, _q = {}, 0
for _kind, _n, _cols in STREAM:
    if _cols == PAIR and _kind != "v":
        PAIR_BASE[_kind] = _q
        _q += _n
GATE_UNITS = [BASE["gates_low"] + i for i in range(2)] + [BASE["gates_high"] + i for i in range(2)]
BRANCH_UNITS = [BASE["gate_br_first"]] + [BASE["gate_br_rest"] + j for j in range(KR // 2 - 1)]
FREED = {"gu0": 0, "qk": KF, "gu1": KF + KD, "gu2": 2 * KF + KD, "gu3": 3 * KF + KD}


def build_trunk(nc, x_t, params, gu, down, qk, f_w, v_w, fox_out, rec, gates, gate_br, lru_out, out_t):
    ctx = ExitStack()
    with ctx:
        base = (nc.sbuf_base + 31) // 32 * 32
        nc_room = nc.sbuf_bytes_remaining
        ctx.enter_context(nc.sbuf_tensor("slab", [P, (nc.sbuf_bytes_remaining - 64) // 4], F32))
        end = [0]

        def place(at, name, cols, dt=F32, parts=P):
            return nc.alloc_sbuf_tensor_at(name, [parts, cols], dt, offset=base + 4 * at)

        def area(cols):
            at = end[0]
            end[0] = at + (cols + 7) // 8 * 8
            return at

        def sb(name, cols, dt=F32, parts=P):
            return place(area(cols), name, cols, dt, parts)

        def sem(name):
            return ctx.enter_context(nc.semaphore(name))

        x = sb("x", KD * T)
        w_raw = [sb(f"w_raw{i}", PAIR) for i in range(2)]
        w_hi = [sb(f"w_hi{i}", PAIR, F32R) for i in range(2)]
        w_lo = [sb(f"w_lo{i}", PAIR, F32R) for i in range(2)]
        par = sb("par", N_PARAMS)
        r_bc = sb("r_bc", T)
        ssq = sb("ssq", T)
        sq_at = area(2 * T)
        sq = place(sq_at, "sq", 2 * T)
        ones = sb("ones", P)
        ident = sb("ident", P)
        ident_r = sb("ident_r", P, F32R)
        mask_r = sb("mask_r", P, F32R)
        eps = sb("eps", 1)
        r_tok = sb("r_tok", TT)
        lru_c = sb("lru_c", KR)
        lru_nc = sb("lru_nc", KR)
        sp = sb("sp", 6 * KR)
        neg_max = sb("neg_max", TT)
        row_sum = sb("row_sum", TT)
        row_rcp = sb("row_rcp", TT)

        xg_area = area(2 * KD * T)
        h_area = area(2 * KF * T)
        t_area = area(4 * T)
        assert 4 * end[0] + 64 <= nc_room, (4 * end[0], nc_room)

        xg_hi = place(xg_area, "xg_hi", KD * T, F32R)
        xg_lo = place(xg_area + KD * T, "xg_lo", KD * T, F32R)
        sq_first = place(h_area, "sq_first", KD * T)
        h_hi = place(h_area, "h_hi", KF * T, F32R)
        h_lo = place(h_area + KF * T, "h_lo", KF * T, F32R)
        g_buf = [place(t_area + i * T, f"g_buf{i}", T) for i in range(2)]
        u_buf = [place(t_area + (2 + i) * T, f"u_buf{i}", T) for i in range(2)]
        q_raw = place(h_area, "q_raw", KD * T)
        k_raw = place(h_area + KD * T, "k_raw", KD * T)
        o_hi = place(h_area, "o_hi", KD * T, F32R)
        o_lo = place(h_area + KD * T, "o_lo", KD * T, F32R)
        at = 2 * KD * T
        v_raw = place(h_area + at, "v_raw", TT * D)
        at += TT * D
        QK1, KK1, QK2, KK2 = (slice(i * T, (i + 1) * T) for i in range(4))
        SET_COLS, V_COLS, BLOCK_COLS = 4 * T, 2 * TT * P, P * TT * (TT + 1) // 2
        SETS = 4
        set_at = [h_area + at + i * SET_COLS for i in range(SETS - 1)] + [xg_area]
        at += (SETS - 1) * SET_COLS
        v_at = [h_area + at, xg_area + SET_COLS]
        at += 2 * V_COLS
        fl_a, fl_b, fl_c = (place(h_area + at + i * T, f"fl_{'abc'[i]}", T, F32, HEADS) for i in range(3))
        prob = place(h_area + at, "prob", BLOCK_COLS)
        at += BLOCK_COLS
        q_low = place(h_area + at, "q_low", T, F32R)
        at += T
        assert at <= 2 * KF * T
        head = [place(set_at[i], f"head{i}", SET_COLS, F32R) for i in range(SETS)]
        v_hi = [place(v_at[i], f"v_hi{i}", V_COLS, F32R) for i in range(2)]
        v_lo = [place(v_at[i] + V_COLS, f"v_lo{i}", V_COLS, F32R) for i in range(2)]
        pt_at = xg_area + SET_COLS + 2 * V_COLS
        PT_COLS = (2 + TT) * 2 * P
        pt_hi = place(pt_at, "pt_hi", PT_COLS, F32R)
        pt_lo = place(pt_at + PT_COLS, "pt_lo", PT_COLS, F32R)
        assert pt_at + 2 * PT_COLS <= xg_area + 2 * KD * T
        f_pack = place(t_area, "f_pack", 2 * T, F32R, 32 + HEADS)
        r_gate = place(h_area, "r_gate", KR * T)
        xc = place(h_area + KR * T, "xc", KR * T)
        xc_hi = place(h_area + 2 * KR * T, "xc_hi", KR * T, F32R)
        xc_lo = place(h_area + 3 * KR * T, "xc_lo", KR * T, F32R)
        q_lru = place(h_area + 2 * KR * T, "q_lru", KR * T)
        gt = place(h_area + 3 * KR * T, "gt", KR * T)
        rec_pad = [place(t_area + i * (T + 8), f"rec_pad{i}", T + TAPS - 1) for i in range(2)]
        a2 = [place(h_area + 4 * KR * T + i * T, f"a2{i}", T) for i in range(4)]
        gi = [place(sq_at + i * T, f"gi{i}", T) for i in range(2)]

        ps = [ctx.enter_context(nc.psum_tensor(f"ps{b}", [P, T], F32)) for b in range(8)]
        BANK_DOWN, BANK_SSQ, BANK_TOK, BANK_F = 4, 6, 7, 5
        BANK_PT, BANK_O, BANK_GATE, BANK_V = 4, 6, 4, 4

        par_in = sem("par_in")
        x_tile_in = [sem(f"x_tile_in{k}") for k in range(KD)]
        raw_in = [sem(f"raw_in{i}") for i in range(2)]
        QUARTERS = 4
        QUARTER = PAIR // QUARTERS
        quarter_in = [sem(f"quarter_in{q}") for q in range(QUARTERS - 1)] + [raw_in[0]]
        quarter_hi = sem("quarter_hi")
        quarter_ready = sem("quarter_ready")
        hi_done = sem("hi_done")
        unit_ready = sem("unit_ready")
        unit_done = sem("unit_done")
        pair_free = sem("pair_free")
        x_new = sem("x_new")
        xg_hi_done = sem("xg_hi_done")
        xg_ready = sem("xg_ready")
        sq_done = sem("sq_done")
        ssq_added = sem("ssq_added")
        ssq_mm = sem("ssq_mm")
        sqrt_done = sem("sqrt_done")
        r_ready = sem("r_ready")
        ssq_zero = sem("ssq_zero")
        consts = sem("consts")
        g_ready = sem("g_ready")
        silu_done = sem("silu_done")
        h_made = sem("h_made")
        h_hi_done = sem("h_hi_done")
        h_ready = sem("h_ready")
        tok_mm = sem("tok_mm")
        tok_sqrt = sem("tok_sqrt")
        tok_ready = sem("tok_ready")
        f_step = sem("f_step")
        f_exp = sem("f_exp")
        f_packed = sem("f_packed")
        head_in = [sem(f"head_in{i}") for i in range(SETS)]
        v_raw_done = sem("v_raw_done")
        pads = sem("pads")
        qk_hi_done = sem("qk_hi_done")
        q_low_done = sem("q_low_done")
        k_low_done = sem("k_low_done")
        v_hi_done = sem("v_hi_done")
        v_ready = sem("v_ready")
        scores_done = sem("scores_done")
        max_done = sem("max_done")
        exp_done = sem("exp_done")
        rcp_done = sem("rcp_done")
        prob_ready = sem("prob_ready")
        pt_done = sem("pt_done")
        pt_hi_done = sem("pt_hi_done")
        pt_ready = sem("pt_ready")
        pv_done = sem("pv_done")
        o_hi_done = sem("o_hi_done")
        o_ready = sem("o_ready")
        lam_exp = sem("lam_exp")
        lam_step = sem("lam_step")
        rec_ready = sem("rec_ready")
        conv_step = sem("conv_step")
        tap0_done = sem("tap0_done")
        xc_hi_done = sem("xc_hi_done")
        xc_ready = sem("xc_ready")
        gate_mm = sem("gate_mm")
        gate_out = sem("gate_out")
        gi_used = sem("gi_used")
        tanh_done = sem("tanh_done")
        a_done = sem("a_done")
        a2_done = sem("a2_done")
        q_done = sem("q_done")
        root_done = sem("root_done")
        b_done = sem("b_done")
        scan_done = sem("scan_done")
        gt_ready = sem("gt_ready")
        gelu_done = sem("gelu_done")
        y_made = sem("y_made")
        y_hi_done = sem("y_hi_done")
        y_ready = sem("y_ready")
        out_made = sem("out_made")
        out_in_dram = sem("out_in_dram")

        def gain(n, m):
            return par[:, bass.ds(m + (COL_GAIN + n * KD), 1)]

        def col(base, m):
            return par[:, base + m:base + m + 1]

        def f32(ap):
            return ap.bitcast(F32)

        def rolled(eng, n, body, first=0, last=0, unroll=2):
            for k in range(first):
                body(k, k % unroll)
            turns = (n - first - last) // unroll
            if turns > 0:
                with eng.Fori(0, turns) as i:
                    for s in range(unroll):
                        body(i * unroll + (first + s), (first + s) % unroll)
            for k in range(first + max(turns, 0) * unroll, n):
                body(k, k % unroll)

        def pair_of(h):
            return h // 2

        def v_of_pair(pair):
            return v_raw[:].rearrange("p (t c n) -> p t c n", t=TT, n=HEAD_DIM)[:, :, bass.ds(pair * 2, 2), :]

        def v_view(ap):
            return ap.rearrange("p (t c n) -> p t c n", t=TT, n=HEAD_DIM)[:, :, 0:4:3, :]

        def pt_block(buf, i):
            at_ = (i // 2) * 4 * P
            return buf[:, at_:at_ + (i + 1) * 2 * P].rearrange("p (j n) -> p j n", j=i + 1)[:, :, (i % 2) * P:(i % 2 + 1) * P]

        HEAD_DMAS = 5

        def halves(h):
            e = h % 2
            return slice(HEAD_DIM * e, HEAD_DIM * (e + 1)), HEAD_DIM * (1 - e)

        def v_low(eng, pair):
            b = pair % 2
            eng.wait_ge(v_hi_done, pair + 1)
            eng.tensor_tensor(v_view(v_lo[b][:]), v_of_pair(pair), v_view(f32(v_hi[b][:])), ALU.subtract)\
                .then_inc(v_ready, 1)

        def ahead(step, h, s, i):
            if not (isinstance(h, int) and h + i // TT >= HEADS):
                step(h + i // TT, s + i // TT, i % TT)

        block = ctx.enter_context(nc.Block())

        @block.sync
        def _(sp_):
            sp_.dma_start(par[:], params).then_inc(par_in, 16)
            for k in range(KD):
                if 2 * k * P % QUARTER == 0:
                    q = 2 * k * P // QUARTER
                    sp_.dma_start(w_raw[0][:, ts(q, QUARTER)], gu[0][0][:, ts(q, QUARTER)]).then_inc(quarter_in[q], 16)
                sp_.dma_start(x[:, ts(k, T)], x_t[k]).then_inc(x_tile_in[k], 16)

            def load(dram, base, cols):
                def body(k, s):
                    u = k + base
                    slot = (base + s) % 2
                    if isinstance(u, int) and u == 0:
                        return
                    if not (isinstance(u, int) and u < 2):
                        sp_.wait_ge(unit_ready, u - 1)
                    sp_.dma_start(w_raw[slot][:, 0:cols],
                                  dram[bass.ds(k, 1)].rearrange("a p n -> (a p) n")).then_inc(raw_in[slot], 16)
                return body

            def move_parts(h):
                ops, (own, other) = head[h % SETS], halves(h)
                if h == 0:
                    sp_.wait_ge(f_packed, 2)
                    sp_.wait_ge(pads, 3 * (SETS - 1))
                elif h == SETS - 1:
                    sp_.wait_ge(pads, 3 * SETS + 2)
                elif h >= SETS:
                    sp_.wait_ge(scores_done, (h - SETS + 1) * TT)
                into = head_in[h % SETS]
                for row, op, cols_ in ((other, QK2, slice(0, T)), (other + 32, KK2, slice(T, 2 * T))):
                    sp_.dma_start(f32(ops[row:row + 2, op]), f32(f_pack[h:h + 33:32, cols_])).then_inc(into, 16)
                sp_.wait_ge(qk_hi_done, 2 * h + 1)
                sp_.dma_start(f32(ops[other:other + HEAD_DIM, KK1]), f32(ops[own, KK1])).then_inc(into, 16)
                sp_.wait_ge(qk_hi_done, 2 * h + 2)
                sp_.dma_start(f32(ops[own, QK2]), f32(ops[own, QK1])).then_inc(into, 16)
                sp_.wait_ge(q_low_done, h + 1)
                sp_.dma_start(f32(ops[other:other + HEAD_DIM, QK1]), f32(q_low[own, :])).then_inc(into, 16)

            for kind, n, cols in STREAM:
                dram = {"qk": qk, "f": f_w, "v": v_w, "fox_out": fox_out, "rec": rec, "lru_out": lru_out,
                        "gates_low": gates[0:2], "gates_high": gates[2:4],
                        "gate_br_first": gate_br[0:1], "gate_br_rest": gate_br[1:KR // 2]}.get(kind)
                if dram is None:
                    dram = (gu if kind.startswith("gu") else down)[int(kind[-1])]
                if kind == "fox_out":
                    for h in range(SETS - 1):
                        move_parts(h)
                    for k in range(n):
                        load(dram, BASE[kind], cols)(k, k)
                        if k == 1:
                            for h in range(SETS - 1, HEADS):
                                move_parts(h)
                else:
                    rolled(sp_, n, load(dram, BASE[kind], cols), first=2 if kind == "gu0" else 0)

            for m in range(KD):
                sp_.wait_ge(out_made, m + 1)
                sp_.dma_start(out_t[m], x[:, ts(m, T)]).then_inc(out_in_dram, 16)
            sp_.wait_ge(out_in_dram, 16 * KD)

        @block.gpsimd
        def _(pool):
            pool.memset(eps[:], EPS).then_inc(consts, 1)
            pool.memset(ones[:], 1.0).then_inc(consts, 1)
            pool.memset(ident[:], 1.0).then_inc(consts, 1)
            pool.memset(f32(mask_r[:]), 0.0).then_inc(consts, 1)
            pool.wait_ge(consts, 4)
            pool.affine_select(out=ident[:], in_=ident[:], compare_op=ALU.is_equal, fill=0.0, base=0,
                               pattern=[[-1, P]], channel_multiplier=1).then_inc(consts, 1)
            pool.affine_select(out=mask_r[:], in_=f32(mask_r[:]), compare_op=ALU.is_ge, fill=MASKED, base=0,
                               pattern=[[-1, P]], channel_multiplier=1).then_inc(consts, 1)
            pool.sem_inc(pt_ready, 2)
            pool.sem_inc(o_ready, 2)

            n_pads = [0]

            def pad(ap, value):
                if n_pads[0]:
                    pool.wait_ge(pads, n_pads[0])
                pool.memset(f32(ap), value).then_inc(pads, 1)
                n_pads[0] += 1

            def pad_head(i):
                other = halves(i)[1]
                pad(head[i][other:other + HEAD_DIM, QK2.start:KK2.stop], 0.0)
                pad(head[i][other + 32:other + 34, QK2], 1.0)
                pad(head[i][other:other + 2, KK2], 1.0)

            def pad_v(i):
                pad(v_hi[i][:], 0.0)
                pad(v_lo[i][:], 0.0)

            def low_parts(h):
                ops, own = head[h % SETS], halves(h)[0]
                if h >= 2:
                    pool.wait_ge(head_in[(h - 2) % SETS], 16 * HEAD_DMAS * ((h - 2) // SETS + 1))
                pool.wait_ge(qk_hi_done, 2 * h + 2)
                pool.tensor_tensor(q_low[own, :], q_raw[own, ts(pair_of(h), T)], f32(ops[own, QK1]), ALU.subtract)\
                    .then_inc(q_low_done, 1)
                pool.tensor_tensor(ops[own, KK2], k_raw[own, ts(pair_of(h), T)], f32(ops[own, KK1]), ALU.subtract)\
                    .then_inc(k_low_done, 1)

            pool.wait_ge(unit_done, BASE["qk"])
            for i in range(SETS - 1):
                pad_head(i)
            pad_v(0)
            pool.wait_ge(pads, 3 * (SETS - 1) + 2)
            pool.wait_ge(f_packed, 2)
            for h in range(SETS - 1):
                low_parts(h)
            pool.wait_ge(unit_done, BASE["fox_out"])
            pool.wait_ge(k_low_done, SETS - 1)
            pad_head(SETS - 1)
            pad_v(1)
            for h in range(SETS - 1, HEADS + 2):
                if h < HEADS:
                    low_parts(h)
                if h % 2 == 0:
                    pool.wait_ge(k_low_done, min(h + 1, HEADS))
                    v_low(pool, h // 2 - 1)
                    pool.wait_ge(v_ready, h // 2)

            for m in range(KR):
                pool.wait_ge(a_done, m + 1)
                if m >= 4:
                    pool.wait_ge(q_done, m - 3)
                pool.tensor_tensor(a2[m % 4][:], r_gate[:, ts(m, T)], r_gate[:, ts(m, T)], ALU.mult).then_inc(a2_done, 1)

        @block.tensor
        def _(pe):
            def mm3(dst, a_hi, a_lo, b_hi, b_lo, start, stop):
                pe.matmul(dst, a_hi, b_hi, start=start, stop=False)
                pe.matmul(dst, a_hi, b_lo, start=False, stop=False)
                return pe.matmul(dst, a_lo, b_hi, start=False, stop=stop)

            def sum_squares(n):
                pe.wait_ge(ssq_added, KD * (n + 1))
                pe.matmul(ps[BANK_SSQ][:], ones[:], ssq[:], start=True, stop=True).then_inc(ssq_mm, 1)

            def pair_unit(base, pair_base, src_hi, src_lo, bank_free, ready=None, after_first=None, in_second=None):
                def body(j, s):
                    u = j + base
                    slot, bank = (base + s) % 2, 2 * ((pair_base + s) % 2)
                    first = isinstance(j, int) and j == 0
                    unit_0 = isinstance(u, int) and u == 0
                    if not unit_0:
                        pe.wait_ge(unit_ready, u + 1)
                    bank_free(j)
                    for k in range(KD):
                        if unit_0 and 2 * k * P % QUARTER == 0:
                            q = 2 * k * P // QUARTER
                            pe.wait_ge(*((quarter_ready, q + 1) if q < QUARTERS - 1 else (unit_ready, 1)))
                        if first and ready:
                            ready(k)
                        if in_second and isinstance(j, int) and j == 1 and k == KD // 2 - 1:
                            in_second()
                        for t in range(2):
                            b = ts(2 * k + t, P)
                            last = mm3(ps[bank + t][:], w_hi[slot][:, b], w_lo[slot][:, b],
                                       src_hi[:, ts(k, T)], src_lo[:, ts(k, T)], k == 0, k == KD - 1)
                    last.then_inc(unit_done, 1)
                    if first and after_first:
                        after_first()
                return body

            def after_two(sem_, before, per_unit):
                def wait(j):
                    if not (isinstance(j, int) and j < 2):
                        pe.wait_ge(sem_, j * per_unit + (before - per_unit))
                return wait

            def xg_wait(n):
                return lambda k: pe.wait_ge(xg_ready, KD * n + k + 1)

            def ffn(f, n):
                gu_k, down_k = f"gu{f}", f"down{f}"
                later = after_two(pair_free, FREED[gu_k], 1)

                def bank_free(j):
                    if f == 1 and isinstance(j, int) and j < 2:
                        pe.wait_ge(x_new, KD * n - KD + KD - 2 + 2 * j)
                    later(j)
                def stats():
                    sum_squares(n)
                rolled(pe, KF, pair_unit(BASE[gu_k], PAIR_BASE[gu_k], xg_hi, xg_lo, bank_free, xg_wait(n),
                                         after_first=stats if f else None, in_second=None if f else stats), first=2)

                def down_tile(m, s):
                    bank = BANK_DOWN + s
                    first = isinstance(m, int) and m == 0
                    for half in range(2):
                        u = m * 2 + (BASE[down_k] + half)
                        slot = (BASE[down_k] + half) % 2
                        pe.wait_ge(unit_ready, u + 1)
                        if half == 0 and not (isinstance(m, int) and m < 2):
                            pe.wait_ge(x_new, m + (KD * n - 1))
                        for kk in range(HALF_F):
                            k = half * HALF_F + kk
                            if first:
                                pe.wait_ge(h_ready, KF * f + k + 1)
                            last = mm3(ps[bank][:], w_hi[slot][:, ts(kk, P)], w_lo[slot][:, ts(kk, P)],
                                       h_hi[:, ts(k, T)], h_lo[:, ts(k, T)], k == 0, k == KF - 1)
                        last.then_inc(unit_done, 1)
                rolled(pe, KD, down_tile, first=2)

            def fox(n):
                def first_stats():
                    sum_squares(n)
                    for tt in range(TT):
                        last = pe.matmul(ps[BANK_TOK][:, tt:tt + 1], ssq[:, ts(tt, P)], ones[:, 0:1],
                                         start=True, stop=True)
                    last.then_inc(tok_mm, 1)
                rolled(pe, KD, pair_unit(BASE["qk"], PAIR_BASE["qk"], xg_hi, xg_lo,
                                         after_two(pair_free, FREED["qk"], 1), xg_wait(n), first_stats), first=2)
                u = BASE["f"]
                pe.wait_ge(unit_ready, u + 1)
                for k in range(KD):
                    last = mm3(ps[BANK_F][:], w_hi[u % 2][:, ts(k, P)], w_lo[u % 2][:, ts(k, P)],
                               xg_hi[:, ts(k, T)], xg_lo[:, ts(k, T)], k == 0, k == KD - 1)
                last.then_inc(unit_done, 1)
                for c in range(2):
                    for half in range(2):
                        u = BASE["v"] + 2 * c + half
                        pe.wait_ge(unit_ready, u + 1)
                        if c == 0 and half == 0:
                            pe.wait_ge(f_step, 1)
                            pe.wait_ge(r_ready, n + 1)
                            pe.wait_ge(tok_ready, 1)
                        if c == 1 and half == 0:
                            pe.wait_ge(pair_free, FREED["qk"] + KD)
                        for kk in range(KD // 2):
                            k = half * (KD // 2) + kk
                            for tt in range(TT):
                                at_ = slice(k * T + tt * P, k * T + (tt + 1) * P)
                                wc = ts(kk, T)
                                last = mm3(ps[BANK_V * (1 - c) + tt][:], xg_hi[:, at_], xg_lo[:, at_],
                                           w_hi[u % 2][:, wc], w_lo[u % 2][:, wc], k == 0, k == KD - 1)
                        last.then_inc(unit_done, 1)

                def scores(h, s, i):
                    ops = head[s % SETS]
                    w = (i + 1) * P
                    if i == 0:
                        pe.wait_ge(head_in[s % SETS], h * 4 * HEAD_DMAS + 4 * HEAD_DMAS * (4 - s % SETS))
                        pe.wait_ge(k_low_done, h + 1)
                    if isinstance(h, int) and h == 0:
                        pe.wait_ge(v_raw_done, 2 * TT)
                    else:
                        pe.wait_ge(exp_done, h * TT + (i + 1 - TT))
                    dst = ps[i][:, 0:w]
                    pe.matmul(dst, ops[:, QK1.start + i * P:QK1.start + w], ops[:, KK1.start:KK1.start + w],
                              start=True, stop=False)
                    pe.matmul(dst, ops[:, QK2.start + i * P:QK2.start + w], ops[:, KK2.start:KK2.start + w],
                              start=False, stop=False)
                    pe.matmul(ps[i][:, i * P:w], ident_r[:], mask_r[:], start=False, stop=True)\
                        .then_inc(scores_done, 1)

                def transposes(h, s, i):
                    at_ = P * (i * (i + 1) // 2)
                    pe.wait_ge(prob_ready, h * TT + (i + 1))
                    pe.wait_ge(pt_ready, h * TT + (i + 1))
                    for j in range(i + 1):
                        last = pe.transpose(ps[BANK_PT + i % 2][:, ts(j, P)], prob[:, at_ + j * P:at_ + (j + 1) * P],
                                            ident[:])
                    last.then_inc(pt_done, 1)

                def values(h, s, i):
                    vb, even = (s // 2) % 2, s % 2 == 0
                    if even and i == 1:
                        pe.wait_ge(v_ready, pair_of(h) + 1)
                        pe.wait_ge(o_ready, pair_of(h) + 1)
                    pe.wait_ge(pt_ready, h * TT + (i + 3))
                    for j in range(i + 1):
                        vc = slice((2 * j + s % 2) * P, (2 * j + s % 2 + 1) * P)
                        q0 = max(i - 1, j)
                        n = (i + 1 - q0) * P
                        at_ = (i // 2) * 4 * P + j * 2 * P + (q0 % 2) * P
                        last = mm3(ps[BANK_O + vb][:, q0 * P:(i + 1) * P], v_hi[vb][:, vc], v_lo[vb][:, vc],
                                   pt_hi[:, at_:at_ + n], pt_lo[:, at_:at_ + n], even and i == 1 and j == 0,
                                   not even and i == TT - 1 and j == i)
                    if i == TT - 1 and not even:
                        last.then_inc(pv_done, 1)

                def attend(h, s):
                    for i in range(TT):
                        ahead(transposes, h, s, i + 1)
                        ahead(scores, h, s, i + 5)
                        if i % 2 == 1:
                            values(h, s, i)

                for i in range(TT):
                    scores(0, 0, i)
                scores(1, 1, 0)
                transposes(0, 0, 0)
                rolled(pe, HEADS, attend, first=1, last=3, unroll=4)

                rolled(pe, KD // 2, pair_unit(BASE["fox_out"], PAIR_BASE["fox_out"], o_hi, o_lo,
                                              after_two(x_new, KD * n, 2),
                                              lambda k: pe.wait_ge(o_ready, k + 3)), first=2)

            def lru(n):
                rolled(pe, KR // 2, pair_unit(BASE["rec"], PAIR_BASE["rec"], xg_hi, xg_lo, after_two(rec_ready, 0, 2),
                                              xg_wait(n), lambda: sum_squares(n)), first=2)

                def gate_tiles(i):
                    u, blk = GATE_UNITS[i], 0
                    pe.wait_ge(unit_ready, u + 1)
                    for m0 in range(GATE_HALF):
                        m, g = (i // 2) * GATE_HALF + m0, i * GATE_HALF + m0
                        if g >= 4:
                            pe.wait_ge(gate_out, g - 3)
                        elif g == 0:
                            pe.wait_ge(r_ready, n + 1)
                        pe.wait_ge(xc_ready, BAND[m][-1] + 1)
                        for t, k in enumerate(BAND[m]):
                            last = mm3(ps[BANK_GATE + g % 4][:], w_hi[u % 2][:, ts(blk, P)], w_lo[u % 2][:, ts(blk, P)],
                                       xc_hi[:, ts(k, T)], xc_lo[:, ts(k, T)], t == 0, t == len(BAND[m]) - 1)
                            blk += 1
                        last.then_inc(unit_done if m0 == GATE_HALF - 1 else gate_mm, 1)

                def branch_free(j):
                    if j < 2:
                        pe.wait_ge(rec_ready, KR - 2 + 2 * j)
                    else:
                        pe.wait_ge(gt_ready, 2 * (j - 1))

                def branch(j):
                    base_ = BRANCH_UNITS[j] - j
                    pair_unit(base_, PAIR_BASE["gate_br_first"], xg_hi, xg_lo, branch_free)(j, j)

                gate_tiles(0)
                gate_tiles(1)
                branch(0)
                gate_tiles(2)
                gate_tiles(3)
                for j in range(1, KR // 2):
                    branch(j)

                def out_tile(m, s):
                    u = m + BASE["lru_out"]
                    slot, bank = (BASE["lru_out"] + s) % 2, BANK_DOWN + s
                    pe.wait_ge(unit_ready, u + 1)
                    if isinstance(m, int) and m < 2:
                        pe.wait_ge(gate_out, 4 * GATE_HALF)
                    else:
                        pe.wait_ge(x_new, m + (KD * n - 1))
                    for k in range(KR):
                        if isinstance(m, int) and m == 0:
                            pe.wait_ge(y_ready, k + 1)
                        last = mm3(ps[bank][:], w_hi[slot][:, ts(k, P)], w_lo[slot][:, ts(k, P)],
                                   xc_hi[:, ts(k, T)], xc_lo[:, ts(k, T)], k == 0, k == KR - 1)
                    last.then_inc(unit_done, 1)
                rolled(pe, KD, out_tile, first=2)

            pe.wait_ge(consts, 7)
            ffn(0, 0)
            fox(1)
            ffn(1, 2)
            ffn(2, 3)
            lru(4)
            ffn(3, 5)
            sum_squares(N_NORMS - 1)

        @block.scalar
        def _(act):
            def hi_split(u, cols, slot):
                if isinstance(u, int):
                    if u >= N_UNITS:
                        return
                    cols = UNIT_COLS[u]
                act.wait_ge(raw_in[slot], u * 8 + (16 - 8 * slot))
                if not (isinstance(u, int) and u < 2):
                    act.wait_ge(unit_done, u - 1)
                act.activation(w_hi[slot][:, 0:cols], w_raw[slot][:, 0:cols], ACT.Copy).then_inc(hi_done, 1)

            def x_tile(n, m, s):
                c = m + KD * n
                if not (isinstance(c, int) and c < 2):
                    act.wait_ge(ssq_added, c - 1)
                act.wait_ge(x_new, m + (KD * (n - 1) + 1))
                if n < N_NORMS - 1:
                    act.activation(xg_hi[:, ts(m, T)], x[:, ts(m, T)], ACT.Copy, scale=gain(n, m))\
                        .then_inc(xg_hi_done, 1)
                act.activation(sq[:, ts(s, T)], x[:, ts(m, T)], ACT.Square).then_inc(sq_done, 1)

            def root(n):
                act.wait_ge(ssq_mm, n + 1)
                act.activation(r_bc[:], ps[BANK_SSQ][:], ACT.Sqrt, scale=1.0 / D, bias=eps[:]).then_inc(sqrt_done, 1)

            def ffn(f, n):
                gu_k, down_k = f"gu{f}", f"down{f}"

                def gu_unit(j, s):
                    if isinstance(j, int) and j == 0 and n:
                        root(n)
                    hi_split(j + (BASE[gu_k] + 2), PAIR, (BASE[gu_k] + s) % 2)
                    if isinstance(j, int) and j == 0 and not n:
                        root(n)
                    act.wait_ge(g_ready, j + (KF * f + 1))
                    act.activation(g_buf[s][:], g_buf[s][:], ACT.Silu).then_inc(silu_done, 1)
                rolled(act, KF, gu_unit, first=2, last=2)

                def down_tile(m, s):
                    u = m * 2 + (BASE[down_k] + 2)
                    hi_split(u, DOWN, BASE[down_k] % 2)
                    x_tile(n + 1, m, s)
                    hi_split(u + 1, DOWN, (BASE[down_k] + 1) % 2)
                rolled(act, KD, down_tile, last=2)

            def fox(n):
                def qk_unit(j, s):
                    if isinstance(j, int) and j == 0:
                        root(n)
                        act.wait_ge(tok_mm, 1)
                        act.activation(r_tok[:], ps[BANK_TOK][:, 0:TT], ACT.Sqrt, scale=1.0 / D, bias=eps[:])\
                            .then_inc(tok_sqrt, 1)
                    hi_split(j + (BASE["qk"] + 2), PAIR, (BASE["qk"] + s) % 2)
                rolled(act, KD, qk_unit, first=2, last=2)
                def k_split(h, e, set_):
                    own = halves(e)[0]
                    act.activation(head[set_][own, KK1], k_raw[own, ts(pair_of(h), T)], ACT.Copy).then_inc(qk_hi_done, 1)

                def q_split(h, e, set_):
                    own = halves(e)[0]
                    act.activation(head[set_][own, QK1], q_raw[own, ts(pair_of(h), T)], ACT.Copy).then_inc(qk_hi_done, 1)

                hi_split(BASE["f"] + 2, 0, BASE["f"] % 2)
                act.wait_ge(f_step, 2)
                act.activation(fl_b[:], fl_a[:], ACT.Abs).then_inc(f_exp, 1)
                act.wait_ge(f_exp, 1)
                act.activation(fl_b[:], fl_b[:], ACT.Exp, scale=-1.0).then_inc(f_exp, 1)
                act.wait_ge(f_exp, 2)
                act.activation(fl_b[:], fl_b[:], ACT.Ln, scale=1.0, bias=ones[0:HEADS, 0:1]).then_inc(f_exp, 1)
                act.wait_ge(pair_free, FREED["qk"] + KD)
                for h in range(SETS - 1):
                    k_split(h, h % 2, h)
                    q_split(h, h % 2, h)
                for i in range(4):
                    u = BASE["v"] + i
                    if i < 3:
                        hi_split(u + 2, 0, u % 2)
                    if i % 2 == 1:
                        c = i // 2
                        act.wait_ge(unit_done, u + 1)
                        act.wait_ge(tok_ready, 1)
                        for tt in range(TT) if c == 0 else range(0, TT, 2):
                            act.activation(v_raw[:, tt * D + c * T:tt * D + (c + 1) * T], ps[BANK_V * (1 - c) + tt][:],
                                           ACT.Copy, scale=r_tok[:, tt:tt + 1]).then_inc(v_raw_done, 1)

                def v_split(pair, b):
                    act.activation(v_view(v_hi[b][:]), v_of_pair(pair), ACT.Copy).then_inc(v_hi_done, 1)

                def exp_block(h, s, i):
                    w, at_ = (i + 1) * P, P * (i * (i + 1) // 2)
                    act.wait_ge(max_done, h * TT + (i + 1))
                    act.activation(prob[:, at_:at_ + w], ps[i][:, 0:w], ACT.Exp, bias=neg_max[:, i:i + 1],
                                   accum_out=row_sum[:, i:i + 1]).then_inc(exp_done, 1)

                def pt_high(h, s, i):
                    w = (i + 1) * P
                    act.wait_ge(pt_done, h * TT + (i + 1))
                    src = ps[BANK_PT + i % 2][:, 0:w].rearrange("p (j n) -> p j n", n=P)
                    act.activation(pt_block(pt_hi, i), src, ACT.Copy).then_inc(pt_hi_done, 1)

                def o_split(pair, b):
                    act.activation(o_hi[:, ts(pair, T)], ps[BANK_O + b][:], ACT.Copy).then_inc(o_hi_done, 1)

                def attend(h, s):
                    nb = (s // 2 + 1) % 2
                    more = not (isinstance(h, int) and h + 2 >= HEADS)
                    for i in range(TT):
                        ahead(exp_block, h, s, i + 3)
                        ahead(pt_high, h, s, i + 1)
                        if i < 2 and not (isinstance(h, int) and h + SETS - 1 >= HEADS):
                            (k_split, q_split)[i](h + (SETS - 1), (s + 1) % 2, (s - 1) % SETS)
                        if (s % 2, i) == (0, 3) and not (isinstance(h, int) and h == 0):
                            o_split(pair_of(h) - 1, nb)
                        if more and (s % 2, i) == (1, 2):
                            v_split(pair_of(h) + 1, nb)

                act.wait_ge(v_raw_done, 2 * TT)
                v_split(0, 0)
                exp_block(0, 0, 0)
                exp_block(0, 0, 1)
                pt_high(0, 0, 0)
                exp_block(0, 0, 2)
                act.wait_ge(pads, 3 * SETS + 4)
                rolled(act, HEADS, attend, first=1, last=3, unroll=4)
                act.wait_ge(pv_done, HEADS // 2)
                o_split(HEADS // 2 - 1, (HEADS // 2 - 1) % 2)
                hi_split(BASE["fox_out"] + 1, 0, (BASE["fox_out"] + 1) % 2)

                def out_unit(j, s):
                    hi_split(j + (BASE["fox_out"] + 2), PAIR, (BASE["fox_out"] + s) % 2)
                    for t in range(2):
                        x_tile(n + 1, j * 2 + t, t)
                rolled(act, KD // 2, out_unit, last=2)

            def lru(n):
                def rec_unit(j, s):
                    if isinstance(j, int) and j == 0:
                        root(n)
                    hi_split(j + (BASE["rec"] + 2), PAIR, (BASE["rec"] + s) % 2)
                    for t in range(2):
                        m = j * 2 + t
                        act.wait_ge(rec_ready, m + 1)
                        act.activation(xc[:, ts(m, T)], rec_pad[t][:, 0:T], ACT.Identity,
                                       scale=par[:, bass.ds(m + COL_CONV_W, 1)],
                                       bias=par[:, bass.ds(m + COL_CONV_B, 1)]).then_inc(tap0_done, 1)
                    if j < KR // 2 - 1:
                        conv_high(j)

                def conv_high(j):
                    for t in range(2):
                        m = j * 2 + t
                        act.wait_ge(conv_step, j * 6 + (5 + t))
                        act.activation(xc_hi[:, ts(m, T)], xc[:, ts(m, T)], ACT.Copy).then_inc(xc_hi_done, 1)

                for j in range(KR // 2):
                    rec_unit(j, j % 2)

                def gate_tiles(i):
                    for m0 in range(GATE_HALF):
                        m, g = (i // 2) * GATE_HALF + m0, i * GATE_HALF + m0
                        if m0 == GATE_HALF - 1:
                            act.wait_ge(unit_done, GATE_UNITS[i] + 1)
                        else:
                            act.wait_ge(gate_mm, i * (GATE_HALF - 1) + m0 + 1)
                        if i % 2 == 0:
                            act.activation(r_gate[:, ts(m, T)], ps[BANK_GATE + g % 4][:], ACT.Sigmoid,
                                           bias=col(COL_B_A, m)).then_inc(gate_out, 1)
                        else:
                            if m >= 2:
                                act.wait_ge(gi_used, m - 1)
                            act.activation(gi[m % 2][:], ps[BANK_GATE + g % 4][:], ACT.Sigmoid,
                                           bias=col(COL_B_I, m)).then_inc(gate_out, 1)
                    if i == 0:
                        conv_high(KR // 2 - 1)
                    hi_split(GATE_UNITS[i] + 2, 0, GATE_UNITS[i] % 2)

                def decay(half):
                    act.wait_ge(gate_out, 2 * GATE_HALF * (half + 1))
                    for m in range(half * GATE_HALF, (half + 1) * GATE_HALF):
                        act.activation(q_lru[:, ts(m, T)], r_gate[:, ts(m, T)], ACT.Tanh, scale=lru_nc[:, m:m + 1])\
                            .then_inc(tanh_done, 1)
                        act.activation(r_gate[:, ts(m, T)], r_gate[:, ts(m, T)], ACT.Exp, scale=lru_c[:, m:m + 1])\
                            .then_inc(a_done, 1)

                def roots(half):
                    for m in range(half * GATE_HALF, (half + 1) * GATE_HALF):
                        act.wait_ge(q_done, m + 1)
                        act.activation(q_lru[:, ts(m, T)], q_lru[:, ts(m, T)], ACT.Sqrt).then_inc(root_done, 1)

                def gelu(m):
                    act.wait_ge(gt_ready, m + 1)
                    act.activation(gt[:, ts(m, T)], gt[:, ts(m, T)], ACT.Gelu_apprx_tanh).then_inc(gelu_done, 1)

                def y_high(m):
                    act.wait_ge(y_made, m + 1)
                    act.activation(xc_hi[:, ts(m, T)], xc[:, ts(m, T)], ACT.Copy).then_inc(y_hi_done, 1)

                def branch(j):
                    hi_split(BRANCH_UNITS[j] + 2, 0, BRANCH_UNITS[j] % 2)

                gate_tiles(0)
                gate_tiles(1)
                decay(0)
                roots(0)
                branch(0)
                gate_tiles(2)
                gate_tiles(3)
                decay(1)
                branch(1)
                roots(1)
                for j, tiles in ((2, range(0, 6)), (3, range(6, 8)), (4, range(8, KR))):
                    branch(j)
                    for m in tiles:
                        gelu(m)
                    for m in tiles:
                        y_high(m)

                def out_tile(m, s):
                    hi_split(m + (BASE["lru_out"] + 2), COLS["lru_out"], (BASE["lru_out"] + s) % 2)
                    x_tile(n + 1, m, s)
                rolled(act, KD, out_tile, last=2)

            act.wait_ge(consts, 6)
            act.activation(ident_r[:], ident[:], ACT.Copy).then_inc(consts, 1)
            act.wait_ge(par_in, 16)
            for m in range(KD):
                if 2 * m * P % QUARTER == 0:
                    q = 2 * m * P // QUARTER
                    act.wait_ge(quarter_in[q], 16)
                    act.activation(w_hi[0][:, ts(q, QUARTER)], w_raw[0][:, ts(q, QUARTER)], ACT.Copy)\
                        .then_inc(quarter_hi if q < QUARTERS - 1 else hi_done, 1)
                act.wait_ge(x_tile_in[m], 16)
                act.activation(xg_hi[:, ts(m, T)], x[:, ts(m, T)], ACT.Copy, scale=gain(0, m)).then_inc(xg_hi_done, 1)
            for m in range(KD):
                if m == KD // 2:
                    hi_split(1, 0, 1)
                act.activation(sq_first[:, ts(m, T)], x[:, ts(m, T)], ACT.Square).then_inc(sq_done, 1)
            act.activation(sp[:, 0:KR], par[:, COL_LAMBDA:COL_LAMBDA + KR], ACT.Abs).then_inc(lam_exp, 1)
            act.wait_ge(lam_exp, 1)
            act.activation(sp[:, KR:2 * KR], sp[:, 0:KR], ACT.Exp, scale=-1.0).then_inc(lam_exp, 1)
            act.wait_ge(consts, 7)
            ffn(0, 0)
            fox(1)
            ffn(1, 2)
            ffn(2, 3)
            lru(4)
            ffn(3, 5)
            root(N_NORMS - 1)

        @block.vector
        def _(dve):
            def lo_split(u, cols, slot):
                if isinstance(u, int):
                    if u >= N_UNITS:
                        return
                    cols = UNIT_COLS[u]
                dve.wait_ge(hi_done, u + 1)
                dve.tensor_tensor(w_lo[slot][:, 0:cols], w_raw[slot][:, 0:cols], f32(w_hi[slot][:, 0:cols]),
                                  ALU.subtract).then_inc(unit_ready, 1)

            def norm_low(n, m):
                c = m + KD * n
                if n < N_NORMS - 1:
                    dve.wait_ge(xg_hi_done, c + 1)
                    dve.scalar_tensor_tensor(out=xg_lo[:, ts(m, T)], in0=x[:, ts(m, T)], scalar=gain(n, m),
                                             in1=f32(xg_hi[:, ts(m, T)]), op0=ALU.mult, op1=ALU.subtract)\
                        .then_inc(xg_ready, 1)

            def add_square(n, m, s, sq=sq):
                c = m + KD * n
                dve.wait_ge(sq_done, c + 1)
                dve.wait_ge(ssq_added, c) if not (isinstance(c, int) and c == 0) else None
                dve.tensor_tensor(ssq[:], ssq[:], sq[:, ts(s, T)], ALU.add).then_inc(ssq_added, 1)

            def update_x(n, m, bank, factor):
                dve.scalar_tensor_tensor(out=x[:, ts(m, T)], in0=ps[bank][:], scalar=factor, in1=x[:, ts(m, T)],
                                         op0=ALU.mult, op1=ALU.add).then_inc(x_new, 1)

            def make_r(n):
                dve.wait_ge(ssq_mm, n + 1)
                if n == 1:
                    dve.wait_ge(tok_mm, 1)
                dve.memset(ssq[:], 0.0).then_inc(ssq_zero, 1)
                dve.wait_ge(sqrt_done, n + 1)
                dve.reciprocal(r_bc[:], r_bc[:]).then_inc(r_ready, 1)
                dve.wait_ge(ssq_zero, n + 2)
                dve.wait_ge(r_ready, n + 1)

            def decay_constants():
                lam = par[:, COL_LAMBDA:COL_LAMBDA + KR]
                e, s_, s2, pl = (sp[:, ts(i, KR)] for i in (1, 2, 3, 4))
                n_step = [0]

                def step(ins):
                    n_step[0] += 1
                    ins.then_inc(lam_step, 1)
                    dve.wait_ge(lam_step, n_step[0])
                dve.wait_ge(lam_exp, 2)
                step(dve.tensor_scalar(s_, e, 2.0, None, ALU.add))
                step(dve.reciprocal(s_, s_))
                step(dve.tensor_tensor(s_, e, s_, ALU.mult))
                step(dve.tensor_tensor(s2, s_, s_, ALU.mult))
                step(dve.tensor_scalar(pl, s2, 1.0 / 17, None, ALU.mult))
                for k in (15, 13, 11, 9, 7, 5, 3):
                    step(dve.scalar_tensor_tensor(out=pl, in0=pl, scalar=1.0 / k, in1=s2, op0=ALU.add, op1=ALU.mult))
                step(dve.scalar_tensor_tensor(out=pl, in0=pl, scalar=1.0, in1=s_, op0=ALU.add, op1=ALU.mult))
                step(dve.tensor_scalar(s2, lam, -1.0, 0.0, ALU.mult, ALU.max))
                step(dve.scalar_tensor_tensor(out=pl, in0=pl, scalar=2.0, in1=s2, op0=ALU.mult, op1=ALU.add))
                step(dve.tensor_scalar(lru_c[:], pl, -RG_C, None, ALU.mult))
                step(dve.tensor_scalar(lru_nc[:], pl, RG_C, None, ALU.mult))

            def ffn(f, n):
                gu_k, down_k = f"gu{f}", f"down{f}"

                def gu_unit(j, s):
                    c = j + KF * f
                    bank = 2 * ((PAIR_BASE[gu_k] + s) % 2)
                    early = isinstance(j, int) and j == 0 and not n
                    if early:
                        lo_split(BASE[gu_k] + 2, PAIR, BASE[gu_k] % 2)
                    if isinstance(j, int) and j == 0:
                        make_r(n)
                    dve.wait_ge(unit_done, j + (BASE[gu_k] + 1))
                    dve.tensor_tensor(g_buf[s][:], ps[bank][:], r_bc[:], ALU.mult).then_inc(g_ready, 1)
                    dve.tensor_tensor(u_buf[s][:], ps[bank + 1][:], r_bc[:], ALU.mult).then_inc(pair_free, 1)
                    if not early:
                        lo_split(j + (BASE[gu_k] + 2), PAIR, (BASE[gu_k] + s) % 2)
                    dve.wait_ge(silu_done, c + 1)
                    dve.wait_ge(pair_free, j + (FREED[gu_k] + 1))
                    dve.tensor_tensor(u_buf[s][:], g_buf[s][:], u_buf[s][:], ALU.mult).then_inc(h_made, 1)
                    dve.wait_ge(h_made, c + 1)
                    dve.tensor_copy(h_hi[:, ts(j, T)], u_buf[s][:]).then_inc(h_hi_done, 1)
                    dve.wait_ge(h_hi_done, c + 1)
                    dve.tensor_tensor(h_lo[:, ts(j, T)], u_buf[s][:], f32(h_hi[:, ts(j, T)]), ALU.subtract)\
                        .then_inc(h_ready, 1)
                    if f == 0 and isinstance(j, int) and j == 1:
                        decay_constants()
                rolled(dve, KF, gu_unit, first=2, last=2)

                def down_tile(m, s):
                    u = m * 2 + (BASE[down_k] + 2)
                    lo_split(u, DOWN, BASE[down_k] % 2)
                    dve.wait_ge(unit_done, u)
                    update_x(n + 1, m, BANK_DOWN + s, 0.5)
                    norm_low(n + 1, m)
                    add_square(n + 1, m, s)
                    lo_split(u + 1, DOWN, (BASE[down_k] + 1) % 2)
                rolled(dve, KD, down_tile, last=2)

            def fox(n):
                def qk_unit(j, s):
                    bank = 2 * ((PAIR_BASE["qk"] + s) % 2)
                    if isinstance(j, int) and j == 0:
                        make_r(n)
                        dve.wait_ge(tok_sqrt, 1)
                        dve.reciprocal(r_tok[:], r_tok[:]).then_inc(tok_ready, 1)
                    dve.wait_ge(unit_done, j + (BASE["qk"] + 1))
                    dve.scalar_tensor_tensor(out=q_raw[:, ts(j, T)], in0=ps[bank][:], scalar=HEAD_DIM ** -0.5,
                                             in1=r_bc[:], op0=ALU.mult, op1=ALU.mult)
                    dve.tensor_tensor(k_raw[:, ts(j, T)], ps[bank + 1][:], r_bc[:], ALU.mult).then_inc(pair_free, 1)
                    lo_split(j + (BASE["qk"] + 2), PAIR, (BASE["qk"] + s) % 2)
                rolled(dve, KD, qk_unit, first=2, last=2)

                dve.wait_ge(unit_done, BASE["f"] + 1)
                hp = slice(0, HEADS)
                dve.tensor_tensor(fl_a[:], ps[BANK_F][hp, :], r_bc[hp, :], ALU.mult).then_inc(f_step, 1)
                dve.wait_ge(f_step, 1)
                dve.tensor_scalar(fl_a[:], fl_a[:], par[hp, COL_B_F:COL_B_F + 1], None, ALU.add).then_inc(f_step, 1)
                lo_split(BASE["f"] + 2, 0, BASE["f"] % 2)
                dve.memset(fl_c[:], 1.0).then_inc(f_step, 1)
                dve.wait_ge(f_exp, 3)
                dve.scalar_tensor_tensor(out=fl_a[:], in0=fl_a[:], scalar=0.0, in1=fl_b[:], op0=ALU.min,
                                         op1=ALU.subtract).then_inc(f_step, 1)
                dve.wait_ge(f_step, 4)
                dve.tensor_tensor_scan(fl_b[:], fl_c[:], fl_a[:], 0.0, ALU.mult, ALU.add).then_inc(f_step, 1)
                dve.wait_ge(f_step, 5)
                high, low = slice(0, HEADS), slice(32, 32 + HEADS)
                dve.tensor_copy(f_pack[high, 0:T], fl_b[:]).then_inc(f_step, 1)
                dve.wait_ge(f_step, 6)
                dve.tensor_tensor(f_pack[low, 0:T], fl_b[:], f32(f_pack[high, 0:T]), ALU.subtract).then_inc(f_step, 1)
                dve.wait_ge(f_step, 7)
                for part in (high, low):
                    dve.tensor_scalar(f_pack[part, T:2 * T], f32(f_pack[part, 0:T]), -1.0, None, ALU.mult)\
                        .then_inc(f_packed, 1)
                for i in range(3):
                    lo_split(BASE["v"] + i + 2, 0, (BASE["v"] + i) % 2)
                dve.wait_ge(unit_done, BASE["v"] + 4)
                for tt in range(1, TT, 2):
                    dve.tensor_scalar(v_raw[:, tt * D + T:tt * D + 2 * T], ps[tt][:], r_tok[:, tt:tt + 1], None, ALU.mult)\
                        .then_inc(v_raw_done, 1)

                def max_block(h, s, i):
                    dve.wait_ge(scores_done, h * TT + (i + 1))
                    dve.tensor_reduce(neg_max[:, i:i + 1], ps[i][:, 0:(i + 1) * P], AX.X, ALU.max,
                                      negate=True).then_inc(max_done, 1)

                def normalise(h, s, i):
                    w, at_ = (i + 1) * P, P * (i * (i + 1) // 2)
                    dve.wait_ge(exp_done, h * TT + (i + 1))
                    dve.reciprocal(row_rcp[:, i:i + 1], row_sum[:, i:i + 1]).then_inc(rcp_done, 1)
                    dve.wait_ge(rcp_done, h * TT + (i + 1))
                    dve.tensor_scalar(prob[:, at_:at_ + w], prob[:, at_:at_ + w], row_rcp[:, i:i + 1], None, ALU.mult)\
                        .then_inc(prob_ready, 1)

                def pt_low(h, s, i):
                    w = (i + 1) * P
                    src = ps[BANK_PT + i % 2][:, 0:w].rearrange("p (j n) -> p j n", n=P)
                    dve.wait_ge(pt_hi_done, h * TT + (i + 1))
                    dve.tensor_tensor(pt_block(pt_lo, i), src, f32(pt_block(pt_hi, i)), ALU.subtract).then_inc(pt_ready, 1)

                def o_split(pair, b):
                    dve.wait_ge(o_hi_done, pair + 1)
                    dve.tensor_tensor(o_lo[:, ts(pair, T)], ps[BANK_O + b][:], f32(o_hi[:, ts(pair, T)]),
                                      ALU.subtract).then_inc(o_ready, 1)

                def attend(h, s):
                    for i in range(TT):
                        ahead(normalise, h, s, i + 2)
                        ahead(max_block, h, s, i + 4)
                        ahead(pt_low, h, s, i + 1)
                        if (s % 2, i) == (0, 3) and not (isinstance(h, int) and h == 0):
                            o_split(pair_of(h) - 1, (s // 2 + 1) % 2)

                v_low(dve, 0)
                max_block(0, 0, 0)
                max_block(0, 0, 1)
                normalise(0, 0, 0)
                max_block(0, 0, 2)
                normalise(0, 0, 1)
                max_block(0, 0, 3)
                pt_low(0, 0, 0)
                rolled(dve, HEADS, attend, first=1, last=3, unroll=4)
                o_split(HEADS // 2 - 1, (HEADS // 2 - 1) % 2)
                lo_split(BASE["fox_out"] + 1, 0, (BASE["fox_out"] + 1) % 2)

                def out_unit(j, s):
                    bank = 2 * ((PAIR_BASE["fox_out"] + s) % 2)
                    dve.wait_ge(unit_done, j + (BASE["fox_out"] + 1))
                    for t in range(2):
                        update_x(n + 1, j * 2 + t, bank + t, 1.0)
                    norm_low(n + 1, j * 2)
                    dve.wait_ge(xg_hi_done, j * 2 + (KD * (n + 1) + 2))
                    m = j * 2 + 1
                    dve.scalar_tensor_tensor(out=xg_lo[:, ts(m, T)], in0=x[:, ts(m, T)], scalar=gain(n + 1, m),
                                             in1=f32(xg_hi[:, ts(m, T)]), op0=ALU.mult, op1=ALU.subtract)\
                        .then_inc(xg_ready, 1)
                    add_square(n + 1, j * 2, 0)
                    add_square(n + 1, m, 1)
                    lo_split(j + (BASE["fox_out"] + 2), PAIR, (BASE["fox_out"] + s) % 2)
                rolled(dve, KD // 2, out_unit, last=2)

            def lru(n):
                dve.memset(rec_pad[0][:, 0:TAPS - 1], 0.0)
                dve.memset(rec_pad[1][:, 0:TAPS - 1], 0.0)

                def rec_unit(j, s):
                    bank = 2 * ((PAIR_BASE["rec"] + s) % 2)
                    if isinstance(j, int) and j == 0:
                        make_r(n)
                    dve.wait_ge(unit_done, j + (BASE["rec"] + 1))
                    for t in range(2):
                        dve.tensor_tensor(rec_pad[t][:, TAPS - 1:TAPS - 1 + T], ps[bank + t][:], r_bc[:], ALU.mult)\
                            .then_inc(rec_ready, 1)
                    lo_split(j + (BASE["rec"] + 2), PAIR, (BASE["rec"] + s) % 2)
                    for tap in range(1, TAPS):
                        for t in range(2):
                            m = j * 2 + t
                            if tap == 1:
                                dve.wait_ge(tap0_done, m + 1)
                            else:
                                dve.wait_ge(conv_step, conv_count(j, tap - 1, t))
                            xm = xc[:, ts(m, T)]
                            dve.scalar_tensor_tensor(out=xm, in0=rec_pad[t][:, tap:tap + T],
                                                     scalar=par[:, bass.ds(m + (COL_CONV_W + tap * KR), 1)],
                                                     in1=xm, op0=ALU.mult, op1=ALU.add).then_inc(conv_step, 1)
                    for t in range(2):
                        m = j * 2 + t
                        dve.wait_ge(xc_hi_done, m + 1)
                        dve.tensor_tensor(xc_lo[:, ts(m, T)], xc[:, ts(m, T)], f32(xc_hi[:, ts(m, T)]), ALU.subtract)\
                            .then_inc(xc_ready, 1)

                def conv_count(j, tap, t):
                    return j * 6 + (2 * (tap - 1) + t + 1)

                for j in range(KR // 2):
                    rec_unit(j, j % 2)

                def gate_tiles(i):
                    if i % 2 == 1:
                        for m in range((i // 2) * GATE_HALF, (i // 2 + 1) * GATE_HALF):
                            dve.wait_ge(gate_out, i * GATE_HALF + m % GATE_HALF + 1)
                            dve.tensor_tensor(xc[:, ts(m, T)], gi[m % 2][:], xc[:, ts(m, T)], ALU.mult).then_inc(gi_used, 1)
                    lo_split(GATE_UNITS[i] + 2, 0, GATE_UNITS[i] % 2)

                def one_minus_a2(m):
                    qm = q_lru[:, ts(m, T)]
                    dve.wait_ge(tanh_done, m + 1)
                    dve.wait_ge(a2_done, m + 1)
                    dve.scalar_tensor_tensor(out=qm, in0=a2[m % 4][:], scalar=1.0, in1=qm, op0=ALU.add, op1=ALU.mult)\
                        .then_inc(q_done, 1)

                def recur(m):
                    xm, qm = xc[:, ts(m, T)], q_lru[:, ts(m, T)]
                    dve.wait_ge(root_done, m + 1)
                    dve.tensor_tensor(xm, qm, xm, ALU.mult).then_inc(b_done, 1)
                    dve.wait_ge(b_done, m + 1)
                    dve.wait_ge(a_done, m + 1)
                    dve.tensor_tensor_scan(qm, r_gate[:, ts(m, T)], xm, 0.0, ALU.mult, ALU.add).then_inc(scan_done, 1)

                def gated(m):
                    dve.wait_ge(scan_done, m + 1)
                    dve.wait_ge(gelu_done, m + 1)
                    dve.tensor_tensor(xc[:, ts(m, T)], q_lru[:, ts(m, T)], gt[:, ts(m, T)], ALU.mult).then_inc(y_made, 1)

                def y_low(m):
                    dve.wait_ge(y_hi_done, m + 1)
                    dve.tensor_tensor(xc_lo[:, ts(m, T)], xc[:, ts(m, T)], f32(xc_hi[:, ts(m, T)]), ALU.subtract)\
                        .then_inc(y_ready, 1)

                def branch(j):
                    bank = 2 * ((PAIR_BASE["gate_br_first"] + j) % 2)
                    dve.wait_ge(unit_done, BRANCH_UNITS[j] + 1)
                    for t in range(2):
                        dve.tensor_tensor(gt[:, ts(2 * j + t, T)], ps[bank + t][:], r_bc[:], ALU.mult).then_inc(gt_ready, 1)
                    lo_split(BRANCH_UNITS[j] + 2, 0, BRANCH_UNITS[j] % 2)

                low, high = range(GATE_HALF), range(GATE_HALF, KR)
                gate_tiles(0)
                gate_tiles(1)
                for m in low:
                    one_minus_a2(m)
                branch(0)
                for m in low:
                    recur(m)
                gate_tiles(2)
                gate_tiles(3)
                for m in high:
                    one_minus_a2(m)
                branch(1)
                for m in high:
                    recur(m)
                for j, tiles in ((2, range(0, 6)), (3, range(6, 8)), (4, range(8, KR))):
                    branch(j)
                    for m in tiles:
                        gated(m)
                    for m in tiles:
                        y_low(m)

                def out_tile(m, s):
                    dve.wait_ge(unit_done, m + (BASE["lru_out"] + 1))
                    update_x(n + 1, m, BANK_DOWN + s, 1.0)
                    norm_low(n + 1, m)
                    add_square(n + 1, m, s)
                    lo_split(m + (BASE["lru_out"] + 2), COLS["lru_out"], (BASE["lru_out"] + s) % 2)
                rolled(dve, KD, out_tile, last=2)

            dve.memset(ssq[:], 0.0).then_inc(ssq_zero, 1)
            dve.wait_ge(par_in, 16)
            dve.wait_ge(ssq_zero, 1)
            for m in range(KD):
                if 2 * m * P % QUARTER == 0:
                    q = 2 * m * P // QUARTER
                    dve.wait_ge(*((quarter_hi, q + 1) if q < QUARTERS - 1 else (hi_done, 1)))
                    dve.tensor_tensor(w_lo[0][:, ts(q, QUARTER)], w_raw[0][:, ts(q, QUARTER)],
                                      f32(w_hi[0][:, ts(q, QUARTER)]), ALU.subtract)\
                        .then_inc(quarter_ready if q < QUARTERS - 1 else unit_ready, 1)
                norm_low(0, m)
            for m in range(KD):
                if m == KD // 2:
                    lo_split(1, 0, 1)
                add_square(0, m, m, sq_first)

            ffn(0, 0)
            fox(1)
            ffn(1, 2)
            ffn(2, 3)
            lru(4)
            ffn(3, 5)
            make_r(N_NORMS - 1)
            for m in range(KD):
                dve.scalar_tensor_tensor(out=x[:, ts(m, T)], in0=x[:, ts(m, T)], scalar=gain(N_NORMS - 1, m),
                                         in1=r_bc[:], op0=ALU.mult, op1=ALU.mult).then_inc(out_made, 1)


def lay_out(a):
    def pairs(w, groups, n):
        if groups == 2:
            return w.reshape(KD, P, 2, n, P).transpose(3, 1, 0, 2, 4).reshape(n, P, PAIR)
        return w.reshape(KD, P, n, 2, P).transpose(2, 1, 0, 3, 4).reshape(n, P, PAIR)

    def interleave(w1, w2):
        return [w[i] for i in range(DEPTH) for w in (w1, w2)]

    cols = []
    norms = [g for i in range(DEPTH) for g in (a["ffn1_norm"][i], a["mix_norm"][i], a["ffn2_norm"][i])]
    for g in norms + [a["final_norm"]]:
        cols.append(g.reshape(KD, P).T)
    cols += [a["lru_conv_w"][0, j].reshape(KR, P).T for j in range(TAPS)]
    cols += [a[k][0].reshape(KR, P).T for k in ("lru_conv_b", "lru_b_a", "lru_b_i", "lru_lambda")]
    b_f = np.zeros((P, 1), np.float32)
    b_f[:HEADS, 0] = a["fox_b_f"][0]
    params = np.concatenate(cols + [b_f], 1)

    w_in = a["fox_w_in"][0]
    f_w = np.zeros((KD, P, P), np.float32)
    f_w[:, :, :HEADS] = w_in[:, 3 * D:].reshape(KD, P, HEADS)
    gates = []
    dense = []
    for w in (a["lru_w_a"][0], a["lru_w_i"][0]):
        full = np.zeros((R, R), np.float32)
        for b in range(LRU_BLOCKS):
            at = slice(b * LRU_BLOCK, (b + 1) * LRU_BLOCK)
            full[at, at] = w[b]
        dense.append(full)
    for half in range(2):
        for full in dense:
            gates.append(np.concatenate([full[k * P:(k + 1) * P, m * P:(m + 1) * P]
                                         for m in range(half * GATE_HALF, (half + 1) * GATE_HALF) for k in BAND[m]], 1))
    lru_in = a["lru_w_in"][0]
    return {
        "x_t": a["x"][0].T.reshape(KD, P, T),
        "params": params,
        "gu": np.stack([pairs(w, 2, KF) for w in interleave(a["ffn1_w_gu"], a["ffn2_w_gu"])]),
        "down": np.stack([w.reshape(2, HALF_F, P, KD, P).transpose(3, 0, 2, 1, 4).reshape(2 * KD, P, DOWN)
                          for w in interleave(a["ffn1_w_down"], a["ffn2_w_down"])]),
        "qk": pairs(w_in[:, :2 * D], 2, KD),
        "f_w": f_w.transpose(1, 0, 2).reshape(1, P, KD * P),
        "v_w": w_in[:, 2 * D:3 * D].reshape(2, KD // 2, P, 2, T).transpose(3, 0, 2, 1, 4).reshape(4, P, PAIR),
        "fox_out": pairs(a["fox_w_out"][0], 1, KD // 2),
        "rec": pairs(lru_in[:, R:], 1, KR // 2),
        "gates": np.stack(gates),
        "gate_br": pairs(lru_in[:, :R], 1, KR // 2),
        "lru_out": a["lru_w_out"][0].reshape(KR, P, KD, P).transpose(2, 1, 0, 3).reshape(KD, P, KR * P),
    }


def kernel(**inputs):
    import concourse.bacc as _bacc
    from concourse.bass_utils import run_bass_kernel_spmd as _run

    nc = _bacc.Bacc("TRN2", target_bir_lowering=False, num_devices=1)
    arrays, args = {}, []
    for name, a in lay_out({k: np.asarray(v) for k, v in inputs.items()}).items():
        a = np.ascontiguousarray(a)
        arrays[f"in_{name}_dram"] = a
        args.append(nc.dram_tensor(f"in_{name}_dram", a.shape, mybir.dt.from_np(a.dtype), kind="ExternalInput").ap())
    args.append(nc.dram_tensor("out_dram", (KD, P, T), F32, kind="ExternalOutput").ap())
    build_trunk(nc, *args)
    r = _run(nc, [arrays], core_ids=[0])
    return np.ascontiguousarray(r.results[0]["out_dram"].reshape(D, T).T)[None]
```
